# Optimizing a Trainium2 kernel written in Bass

```python
import math
import jax, jax.numpy as jnp
from jax import lax
import numpy as np

D_MODEL = 2048
BATCH = 1
SEQ = 512
DEPTH = 1

HEAD_DIM = 64
MIX_WIDTH = D_MODEL
NSA_HEADS = MIX_WIDTH // 2 // HEAD_DIM
NSA_KV_HEADS = NSA_HEADS // 4
NSA_GROUP = NSA_HEADS // NSA_KV_HEADS
SWA_HEADS = (MIX_WIDTH - NSA_HEADS * HEAD_DIM) // HEAD_DIM
SWA_KV_HEADS = SWA_HEADS // 8
SWA_GROUP = SWA_HEADS // SWA_KV_HEADS
CMP_LEN = 32
CMP_STRIDE = 16
CMP_HIDDEN = 4 * HEAD_DIM
SEL_BLOCK = 64
N_SEL = 16
NSA_WINDOW = 512
SWA_WINDOW = 128
NUM_BUCKETS = 32
REL_MAX_DISTANCE = 1024
N_BIAS_HEADS = NSA_HEADS + SWA_HEADS
D_FF = -(-8 * D_MODEL // (3 * 256)) * 256
QBLOCK = 128
RMS_EPS = 1e-5
NEG_INF = -1e30
FORCE_SCORE = 1e6

SPLIT_SIZES = (
    NSA_HEADS * HEAD_DIM,
    NSA_KV_HEADS * HEAD_DIM, NSA_KV_HEADS * HEAD_DIM,
    NSA_KV_HEADS * HEAD_DIM, NSA_KV_HEADS * HEAD_DIM,
    NSA_KV_HEADS * HEAD_DIM, NSA_KV_HEADS * HEAD_DIM,
    NSA_HEADS * 3,
    SWA_HEADS * HEAD_DIM,
    SWA_KV_HEADS * HEAD_DIM, SWA_KV_HEADS * HEAD_DIM,
)
PROJ_WIDTH = sum(SPLIT_SIZES)

kernel_name = "hybrid_nsa_swa_sink_t5bias_swiglu"

def rms_norm(x, g):
    xf = x.astype(jnp.float32)
    y = xf * lax.rsqrt(jnp.mean(xf * xf, axis=-1, keepdims=True) + RMS_EPS)
    return (y * g.astype(jnp.float32)).astype(x.dtype)

def t5_bucket(dist):
    dist = jnp.maximum(dist, 0)
    max_exact = NUM_BUCKETS // 2
    d = jnp.maximum(dist, 1).astype(jnp.float32)
    ratio = jnp.log(d / max_exact) / math.log(REL_MAX_DISTANCE / max_exact)
    large = max_exact + (ratio * (NUM_BUCKETS - max_exact)).astype(jnp.int32)
    large = jnp.minimum(large, NUM_BUCKETS - 1)
    return jnp.where(dist < max_exact, dist, large)

def masked_softmax(s, mask):
    s = jnp.where(mask, s, NEG_INF)
    p = jax.nn.softmax(s, axis=-1)
    return jnp.where(mask, p, 0.0)

def split_columns(proj):
    parts, off = [], 0
    for size in SPLIT_SIZES:
        parts.append(proj[..., off:off + size])
        off += size
    return parts

def to_heads(t, n_heads):
    return t.reshape(t.shape[0], t.shape[1], n_heads, HEAD_DIM)

def compress(kv, pos_emb, w1, w2):
    b, t, hkv, dh = kv.shape
    n_cmp = (t - CMP_LEN) // CMP_STRIDE + 1
    idx = jnp.arange(n_cmp)[:, None] * CMP_STRIDE + jnp.arange(CMP_LEN)[None, :]
    blocks = kv[:, idx] + pos_emb[:, None, :]
    flat = blocks.transpose(0, 1, 3, 2, 4).reshape(b, n_cmp, hkv, CMP_LEN * dh)
    return jax.nn.gelu(flat @ w1) @ w2

def nsa_attention(q, k_c, v_c, k_s, v_s, k_w, v_w, gates, tbl,
                  pos_k, pos_v, ck1, ck2, cv1, cv2):
    b, t = q.shape[0], q.shape[1]
    hkv, grp, dh = NSA_KV_HEADS, NSA_GROUP, HEAD_DIM
    scale = dh ** -0.5
    kc = compress(k_c, pos_k, ck1, ck2)
    vc = compress(v_c, pos_v, cv1, cv2)
    n_cmp = kc.shape[1]
    n_blk = t // SEL_BLOCK
    n_sel = min(N_SEL, n_blk)
    c_end = jnp.arange(n_cmp) * CMP_STRIDE + CMP_LEN - 1
    ci = jnp.arange(n_cmp)[:, None] * CMP_STRIDE
    sj = jnp.arange(n_blk)[None, :] * SEL_BLOCK
    overlap = ((ci < sj + SEL_BLOCK) & (ci + CMP_LEN > sj)).astype(jnp.float32)
    ks_blocks = k_s.reshape(b, n_blk, SEL_BLOCK, hkv, dh).transpose(0, 3, 1, 2, 4)
    vs_blocks = v_s.reshape(b, n_blk, SEL_BLOCK, hkv, dh).transpose(0, 3, 1, 2, 4)
    kwp = jnp.pad(k_w, ((0, 0), (NSA_WINDOW, 0), (0, 0), (0, 0)))
    vwp = jnp.pad(v_w, ((0, 0), (NSA_WINDOW, 0), (0, 0), (0, 0)))
    tbl_g = tbl.reshape(NUM_BUCKETS, hkv, grp)
    tbl_h = tbl_g.transpose(1, 2, 0).astype(jnp.float32)
    b_i = jnp.arange(b)[:, None, None, None]
    h_i = jnp.arange(hkv)[None, :, None, None]
    blk_ids = jnp.arange(n_blk)

    def block(qb):
        t0 = qb * QBLOCK
        tq = t0 + jnp.arange(QBLOCK)
        qblk = lax.dynamic_slice_in_dim(q, t0, QBLOCK, 1).reshape(b, QBLOCK, hkv, grp, dh)
        gblk = lax.dynamic_slice_in_dim(gates, t0, QBLOCK, 1).reshape(b, QBLOCK, hkv, grp, 3)

        dist_c = tq[:, None] - c_end[None, :]
        s_c = jnp.einsum('bqhgd,bchd->bhgqc', qblk, kc).astype(jnp.float32) * scale
        s_c = s_c + tbl_g[t5_bucket(dist_c)].transpose(2, 3, 0, 1).astype(jnp.float32)
        p_c = masked_softmax(s_c, dist_c >= 0)
        o_c = jnp.einsum('bhgqc,bchd->bqhgd', p_c.astype(vc.dtype), vc)

        imp = jnp.einsum('bhgqc,cs->bhqs', p_c, overlap)
        blk_t = tq // SEL_BLOCK
        forced = ((blk_ids[None, :] == 0) | (blk_ids[None, :] == blk_t[:, None])
                  | (blk_ids[None, :] == blk_t[:, None] - 1))
        imp = jnp.where(forced, imp + FORCE_SCORE, imp)
        imp = jnp.where(blk_ids[None, :] > blk_t[:, None], NEG_INF, imp)
        _, top = lax.top_k(imp, n_sel)
        n_tok = n_sel * SEL_BLOCK
        kg = ks_blocks[b_i, h_i, top].reshape(b, hkv, QBLOCK, n_tok, dh)
        vg = vs_blocks[b_i, h_i, top].reshape(b, hkv, QBLOCK, n_tok, dh)
        pos_s = (top[..., None] * SEL_BLOCK + jnp.arange(SEL_BLOCK)).reshape(b, hkv, QBLOCK, n_tok)
        dist_s = tq[None, None, :, None] - pos_s
        s_s = jnp.einsum('bqhgd,bhqkd->bhgqk', qblk, kg).astype(jnp.float32) * scale
        bias_s = tbl_h[jnp.arange(hkv)[None, :, None, None, None],
                       jnp.arange(grp)[None, None, :, None, None],
                       t5_bucket(dist_s)[:, :, None]]
        p_s = masked_softmax(s_s + bias_s, (dist_s >= 0)[:, :, None])
        o_s = jnp.einsum('bhgqk,bhqkd->bqhgd', p_s.astype(vg.dtype), vg)

        kwin = lax.dynamic_slice_in_dim(kwp, t0, QBLOCK + NSA_WINDOW, 1)
        vwin = lax.dynamic_slice_in_dim(vwp, t0, QBLOCK + NSA_WINDOW, 1)
        pos_w = t0 - NSA_WINDOW + jnp.arange(QBLOCK + NSA_WINDOW)
        dist_w = tq[:, None] - pos_w[None, :]
        mask_w = (dist_w >= 0) & (dist_w < NSA_WINDOW) & (pos_w[None, :] >= 0)
        s_w = jnp.einsum('bqhgd,bkhd->bhgqk', qblk, kwin).astype(jnp.float32) * scale
        s_w = s_w + tbl_g[t5_bucket(dist_w)].transpose(2, 3, 0, 1).astype(jnp.float32)
        p_w = masked_softmax(s_w, mask_w)
        o_w = jnp.einsum('bhgqk,bkhd->bqhgd', p_w.astype(vwin.dtype), vwin)

        o = gblk[..., 0:1] * o_c + gblk[..., 1:2] * o_s + gblk[..., 2:3] * o_w
        return o.reshape(b, QBLOCK, hkv * grp * dh)

    out = lax.map(block, jnp.arange(t // QBLOCK))
    return out.transpose(1, 0, 2, 3).reshape(b, t, -1)

def swa_sink_attention(q, k, v, sinks, tbl):
    b, t = q.shape[0], q.shape[1]
    hkv, grp, dh = SWA_KV_HEADS, SWA_GROUP, HEAD_DIM
    scale = dh ** -0.5
    kp = jnp.pad(k, ((0, 0), (SWA_WINDOW, 0), (0, 0), (0, 0)))
    vp = jnp.pad(v, ((0, 0), (SWA_WINDOW, 0), (0, 0), (0, 0)))
    tbl_g = tbl.reshape(NUM_BUCKETS, hkv, grp)
    sink = sinks.reshape(hkv, grp)[None, :, :, None, None].astype(jnp.float32)

    def block(qb):
        t0 = qb * QBLOCK
        tq = t0 + jnp.arange(QBLOCK)
        qblk = lax.dynamic_slice_in_dim(q, t0, QBLOCK, 1).reshape(b, QBLOCK, hkv, grp, dh)
        kwin = lax.dynamic_slice_in_dim(kp, t0, QBLOCK + SWA_WINDOW, 1)
        vwin = lax.dynamic_slice_in_dim(vp, t0, QBLOCK + SWA_WINDOW, 1)
        pos = t0 - SWA_WINDOW + jnp.arange(QBLOCK + SWA_WINDOW)
        dist = tq[:, None] - pos[None, :]
        mask = (dist >= 0) & (dist < SWA_WINDOW) & (pos[None, :] >= 0)
        s = jnp.einsum('bqhgd,bkhd->bhgqk', qblk, kwin).astype(jnp.float32) * scale
        s = s + tbl_g[t5_bucket(dist)].transpose(2, 3, 0, 1).astype(jnp.float32)
        s = jnp.where(mask, s, NEG_INF)
        m = jnp.maximum(jnp.max(s, axis=-1, keepdims=True), sink)
        e = jnp.exp(s - m)
        p = e / (jnp.sum(e, axis=-1, keepdims=True) + jnp.exp(sink - m))
        o = jnp.einsum('bhgqk,bkhd->bqhgd', p.astype(vwin.dtype), vwin)
        return o.reshape(b, QBLOCK, hkv * grp * dh)

    out = lax.map(block, jnp.arange(t // QBLOCK))
    return out.transpose(1, 0, 2, 3).reshape(b, t, -1)

def setup_inputs(seed: int = 0) -> dict:
    key = jax.random.key(seed)
    ks = jax.random.split(key, 18)
    f32 = jnp.float32
    nrm = lambda k, shape, s: jax.random.normal(k, shape, f32) * s
    return {
        "x": nrm(ks[0], (BATCH, SEQ, D_MODEL), 1.0),
        "rel_bias": nrm(ks[1], (NUM_BUCKETS, N_BIAS_HEADS), 0.5),
        "norm_mix": 1.0 + nrm(ks[2], (DEPTH, D_MODEL), 0.02),
        "norm_ffn": 1.0 + nrm(ks[3], (DEPTH, D_MODEL), 0.02),
        "w_in": nrm(ks[4], (DEPTH, D_MODEL, PROJ_WIDTH), D_MODEL ** -0.5),
        "b_in": nrm(ks[5], (DEPTH, PROJ_WIDTH), 0.02),
        "cmp_pos_k": nrm(ks[6], (DEPTH, CMP_LEN, HEAD_DIM), 0.1),
        "cmp_pos_v": nrm(ks[7], (DEPTH, CMP_LEN, HEAD_DIM), 0.1),
        "cmp_k_w1": nrm(ks[8], (DEPTH, CMP_LEN * HEAD_DIM, CMP_HIDDEN), (CMP_LEN * HEAD_DIM) ** -0.5),
        "cmp_k_w2": nrm(ks[9], (DEPTH, CMP_HIDDEN, HEAD_DIM), CMP_HIDDEN ** -0.5),
        "cmp_v_w1": nrm(ks[10], (DEPTH, CMP_LEN * HEAD_DIM, CMP_HIDDEN), (CMP_LEN * HEAD_DIM) ** -0.5),
        "cmp_v_w2": nrm(ks[11], (DEPTH, CMP_HIDDEN, HEAD_DIM), CMP_HIDDEN ** -0.5),
        "sinks": nrm(ks[12], (DEPTH, SWA_HEADS), 1.0),
        "w_out": nrm(ks[13], (DEPTH, MIX_WIDTH, D_MODEL), MIX_WIDTH ** -0.5),
        "w_gate": nrm(ks[14], (DEPTH, D_MODEL, D_FF), D_MODEL ** -0.5),
        "w_up": nrm(ks[15], (DEPTH, D_MODEL, D_FF), D_MODEL ** -0.5),
        "w_down": nrm(ks[16], (DEPTH, D_FF, D_MODEL), D_FF ** -0.5),
        "norm_final": 1.0 + nrm(ks[17], (D_MODEL,), 0.02),
    }

def reference(x, rel_bias, norm_mix, norm_ffn, w_in, b_in, cmp_pos_k, cmp_pos_v,
              cmp_k_w1, cmp_k_w2, cmp_v_w1, cmp_v_w2, sinks, w_out, w_gate, w_up,
              w_down, norm_final):
    tbl_a = rel_bias[:, :NSA_HEADS]
    tbl_b = rel_bias[:, NSA_HEADS:]
    for layer in range(DEPTH):
        h = rms_norm(x, norm_mix[layer])
        proj = h @ w_in[layer] + b_in[layer]
        q_a, k_c, v_c, k_s, v_s, k_w, v_w, g_a, q_b, k_b, v_b = split_columns(proj)
        gates = jax.nn.sigmoid(g_a).reshape(g_a.shape[0], g_a.shape[1], NSA_HEADS, 3)
        o_a = nsa_attention(
            to_heads(q_a, NSA_HEADS),
            to_heads(k_c, NSA_KV_HEADS), to_heads(v_c, NSA_KV_HEADS),
            to_heads(k_s, NSA_KV_HEADS), to_heads(v_s, NSA_KV_HEADS),
            to_heads(k_w, NSA_KV_HEADS), to_heads(v_w, NSA_KV_HEADS),
            gates, tbl_a,
            cmp_pos_k[layer], cmp_pos_v[layer],
            cmp_k_w1[layer], cmp_k_w2[layer], cmp_v_w1[layer], cmp_v_w2[layer])
        o_b = swa_sink_attention(
            to_heads(q_b, SWA_HEADS), to_heads(k_b, SWA_KV_HEADS),
            to_heads(v_b, SWA_KV_HEADS), sinks[layer], tbl_b)
        x = x + jnp.concatenate([o_a, o_b], axis=-1) @ w_out[layer]
        h = rms_norm(x, norm_ffn[layer])
        x = x + (jax.nn.silu(h @ w_gate[layer]) * (h @ w_up[layer])) @ w_down[layer]
    return rms_norm(x, norm_final)


_drawn_inputs = setup_inputs


def setup_inputs(seed=0):
    import zlib

    import numpy as np

    out = dict(_drawn_inputs(seed))
    spreads = {}
    factors = {'norm_mix': 8.0,
     'norm_ffn': 4.053,
     'b_in': 2.941,
     'cmp_pos_k': 8.0,
     'sinks': 28.849,
     'norm_final': 8.004,
     'cmp_pos_v': 8.0}
    for name, (base, spread) in spreads.items():
        noise = np.random.default_rng([zlib.crc32(name.encode()), seed]).standard_normal(out[name].shape)
        drawn = base * np.exp(spread * noise) if base else spread * noise
        out[name] = __import__('jax').numpy.asarray(drawn.astype(out[name].dtype))
    for name, factor in factors.items():
        out[name] = (out[name] * factor).astype(out[name].dtype)
    return out
```

```python
import math
from contextlib import ExitStack

import numpy as np

import concourse.bass as bass
from concourse import mybir

F32 = mybir.dt.float32
F32R = mybir.dt.float32r
ALU = mybir.AluOpType
ACT = mybir.ActivationFunctionType
AX = mybir.AxisListType

P = 128
SEQ = 512
D_MODEL = 2048
HEAD_DIM = 64
NSA_HEADS = 16
NSA_KV = 4
SWA_HEADS = 16
HEADS = NSA_HEADS + SWA_HEADS
CMP_LEN = 32
CMP_STRIDE = 16
CMP_HIDDEN = 4 * HEAD_DIM
SWA_WINDOW = 128
NUM_BUCKETS = 32
REL_MAX_DISTANCE = 1024
D_FF = 5632
RMS_EPS = 1e-5
MASKED = 1e30
SCALE = HEAD_DIM ** -0.5

KT = D_MODEL // P
TT = SEQ // P
N_CMP = (SEQ - CMP_LEN) // CMP_STRIDE + 1
UNIT_KT = 4
UNIT_COLS = 512
UNIT = UNIT_KT * UNIT_COLS
RAW = 4
RING = 2
FF_BLOCKS = D_FF // UNIT_COLS

Q_A, Q_B, K_S, V_S, K_W, V_W, K_B, V_B, K_C, V_C, GATE = 0, 8, 16, 18, 20, 22, 24, 25, 26, 28, 30
PROJ_TILES = 31
N_GATES = 3 * NSA_HEADS

IN_RUNS = [(0, 512, Q_A), (512, 512, Q_A + 4), (1024, 512, K_C), (1536, 512, K_S), (2048, 512, K_W),
           (2608, 512, Q_B), (3120, 512, Q_B + 4), (3632, 256, K_B), (2560, P, GATE)]

P_OFF = [0, 128, 384, 768]
NSA_COLS = 1280


def bucket_of_distance():
    exact = NUM_BUCKETS // 2
    d = np.arange(SEQ)
    ratio = np.log(np.maximum(d, 1).astype(np.float32) / np.float32(exact)) / np.float32(
        math.log(REL_MAX_DISTANCE / exact))
    large = exact + (ratio * np.float32(NUM_BUCKETS - exact)).astype(np.int32)
    return np.where(d < exact, d, np.minimum(large, NUM_BUCKETS - 1))


def in_units():
    units = []
    for g, (c0, n, tile) in enumerate(IN_RUNS):
        kt = UNIT // n
        units += [(g, k, kt, c0, n, tile) for k in range(0, KT, kt)]
    return units


IN_UNITS = in_units()
N_IN = len(IN_UNITS)
OUT0 = N_IN
N_OUT = 4 * (D_MODEL // UNIT_COLS)
FF0 = OUT0 + N_OUT
LOOP0 = FF0 + 8
PER_BLOCK = 12
TAIL0 = LOOP0 + PER_BLOCK * (FF_BLOCKS - 1)
N_UNITS = TAIL0 + 4
IN_GROUPS = len(IN_RUNS)
IN_LAST = [max(n for n, u in enumerate(IN_UNITS) if u[0] == g) for g in range(IN_GROUPS)]
IN_TILES = [n // P for _, n, _ in IN_RUNS]
OUT_GROUP0 = IN_GROUPS
FF_GROUP0 = OUT_GROUP0 + 4
LOOP_GROUP0 = FF_GROUP0 + 2
GROUPS_PER_BLOCK = 6
TAIL_GROUP0 = LOOP_GROUP0 + GROUPS_PER_BLOCK * (FF_BLOCKS - 1)




def tiles_before(group):
    return sum(IN_TILES[:group]) + 4 * max(0, group - IN_GROUPS)


ITEMS = []
for _pair in range(NSA_HEADS // 2):
    ITEMS += [("c", 2 * _pair)] + [(_b, 2 * _pair + _o) for _b in "sw" for _o in (0, 1)]
for _h in range(NSA_HEADS, HEADS):
    ITEMS += [("b", _h)]
N_ITEMS = len(ITEMS)
ROUNDS = HEADS // 4


def counts(per_item):
    total = [0]
    for item in ITEMS:
        total.append(total[-1] + per_item(item))
    return total


EXP_BEFORE = counts(lambda it: {"c": 1, "b": 5}.get(it[0], 4))
NORM_BEFORE = counts(lambda it: 1 if it[0] == "c" else 4)
COPY_BEFORE = counts(lambda it: {"c": 1, "b": 2}.get(it[0], 3))
HEAD_INDEX = counts(lambda it: it[0] != "c")
PV_RUNS = [x for x, (kind, h) in enumerate(ITEMS) if kind == "c" or h % 2]
PV_BEFORE = counts(lambda it: 1 if it[0] == "c" or it[1] % 2 else 0)
OUT_AFTER = [x for x, (kind, h) in enumerate(ITEMS) if kind in "wb" and h % 2]


def first_item(round_):
    return next(x for x, (_, h) in enumerate(ITEMS) if h // 4 == round_)


def last_item(head):
    return max(x for x, (kind, h) in enumerate(ITEMS) if h == head or (kind == "c" and h == head))


def key_columns(kind, i):
    if kind == "b":
        return (0, [0]) if i == 0 else (P + 2 * P * (i - 1), [i - 1, i])
    return P * i * (i + 1) // 2, list(range(i + 1))


T_BANK = {"n": [(0, 0), (1, 0), (2, 0), (1, 384)], "b": [(0, 0), (0, 256), (1, 0), (1, 256)]}
T_SBUF = {"n": [0, 512, 1024, 896], "b": [0, 256, 512, 768]}
T_COPIES = {"n": [(0, 0, 512), (1, 512, 512), (2, 1024, 256)], "b": [(0, 0, 512), (1, 512, 384)]}

ITEM_OF = [x for x, (kind, _) in enumerate(ITEMS) if kind != "c"]
STACK_BEFORE = [0]
for _r in range(ROUNDS):
    STACK_BEFORE.append(STACK_BEFORE[-1] + (8 if 4 * _r < NSA_HEADS else 6))

PREP_STEPS = ["v0", "v1", "v2", "v3", "v4", "gates", "hidden0", "hidden1", "hidT0", "hidT1", "kc",
              "vc"]
PREP = {name: n + 1 for n, name in enumerate(PREP_STEPS)}
BIAS_W = SEQ + P


def build(nc, x, rel_bias, norm_mix, norm_ffn, w_in, b_in, cmp_pos_k, cmp_pos_v, cmp_k_w1,
          cmp_k_w2, cmp_v_w1, cmp_v_w2, sinks, w_out, w_gate, w_up, w_down, norm_final, out):
    x, out, b_in = x[0], out[0], b_in[0]
    w_in, w_out, w_gate, w_up, w_down = w_in[0], w_out[0], w_gate[0], w_up[0], w_down[0]
    xT_dram = nc.dram_tensor("xT_scratch", [KT, P, SEQ], F32).ap()
    bias_dram = nc.dram_tensor("bias_scratch", [HEADS, P, BIAS_W], F32)

    with ExitStack() as ctx:
        def sb(name, shape, dt=F32):
            return ctx.enter_context(nc.sbuf_tensor(name, shape, dt))

        def sem(name):
            return ctx.enter_context(nc.semaphore(name))

        act_hi = sb("act_hi", [P, KT, SEQ], F32R)
        act_lo = sb("act_lo", [P, KT, SEQ], F32R)
        proj_q = sb("proj_q", [P, K_S, SEQ])
        raw = sb("raw", [P, RAW, UNIT])
        w_hi = sb("w_hi", [P, RING, UNIT], F32R)
        w_lo = sb("w_lo", [P, RING, UNIT], F32R)
        work = sb("work", [P, 2048])
        ident = sb("ident", [P, P])
        ones = sb("ones", [P, P])
        vecs = sb("vecs", [P, P])
        gates = sb("gates", [P, TT, N_GATES])
        kc_hi = sb("kc_hi", [P, NSA_KV, 32], F32R)
        kc_lo = sb("kc_lo", [P, NSA_KV, 32], F32R)
        stats = sb("stats", [P, 4, 3, TT])
        cstats = sb("cstats", [P, 3, 2 * TT])
        sink_sb = sb("sink_sb", [P, 2, SWA_HEADS])
        valid = sb("valid", [P, 1])
        w2k = sb("w2k", [P, 2, 2, HEAD_DIM])
        w2v = sb("w2v", [P, 2, HEAD_DIM])
        squares_by_row = sb("squares_by_row", [P, TT, 4])
        with nc.sbuf_tensor("proj_kv", [P, PROJ_TILES - K_S, SEQ], F32) as proj_kv:
            pass
        ff_hi = sb("ff_hi", [P, UNIT_KT, SEQ], F32R)
        ff_lo = sb("ff_lo", [P, UNIT_KT, SEQ], F32R)
        ff_gate = sb("ff_gate", [P, UNIT_KT, SEQ])
        ff_stage = sb("ff_stage", [P, 3, SEQ])
        banks = [ctx.enter_context(nc.psum_tensor(f"bank{i}", [P, SEQ], F32)) for i in range(8)]
        SETS = [banks[0:4], banks[4:8]]

        def tile_of(t):
            return proj_q[:, t, :] if t < K_S else proj_kv[:, t - K_S, :]

        x_chunk = [proj_kv[:, 4 * s:4 * s + 4, :] for s in range(2)]
        x_stage = [proj_kv[:, 8 + s, :] for s in range(2)]
        xg_stage = [proj_kv[:, 10 + s, :] for s in range(2)]
        bias_rows = proj_kv[0:HEADS, 12:15, :].rearrange("p a b -> p (a b)")
        rel_rows = proj_q[0:HEADS, 9, 0:NUM_BUCKETS]
        rel_t = proj_q[0:HEADS, 9, 128:128 + NUM_BUCKETS]
        vec_rows = proj_q[:, 10, 0:P]
        square = [work[:, 0:512], work[:, 512:1024]]
        sumsq = work[:, 1024:1536]
        rstd = work[:, 1536:2048]
        raw_flat = raw[:, :, :].rearrange("p a b -> p (a b)")
        w1 = [raw_flat[:, 4096 * s:4096 * (s + 1)].rearrange("p (j m) -> p j m", m=CMP_HIDDEN)
              for s in range(2)]
        blocks = work[:, 0:16 * NSA_KV * N_CMP].rearrange("p (j h n) -> p j h n", j=16, h=NSA_KV)
        ROWS_C = NSA_KV * N_CMP
        hidden = [tile_of(K_C + s)[0:ROWS_C, 0:CMP_HIDDEN] for s in range(2)]
        hid_k = tile_of(K_C)[:, 256:256 + 2 * ROWS_C].rearrange("p (k n) -> p k n", k=2)
        hid_v = raw_flat[:, 0:2 * NSA_KV * 4 * 32].rearrange(
            "p (k h r c) -> p k h r c", k=2, h=NSA_KV, r=4)
        vc_pad = work[:, 0:NSA_KV * 4 * HEAD_DIM].rearrange("p (k h d) -> p k h d", k=NSA_KV, h=4)
        pT = [raw_flat[:, NSA_COLS * s:NSA_COLS * (s + 1)] for s in range(4)]
        tables = raw_flat[:, 5120:7168].rearrange("p (s c) -> p s c", s=4)
        pcT = raw_flat[:, 7168:7680]
        prob_c = raw_flat[:, 7680:8192].rearrange("p (i h c) -> p i h c", i=TT, h=4)
        prob_flat = proj_kv[:, K_C - K_S:PROJ_TILES - K_S, :].rearrange("p a b -> p (a b)")
        prob = [prob_flat[:, NSA_COLS * s:NSA_COLS * (s + 1)] for s in range(2)]
        score_c = work[:, 1024:1280].rearrange("p (i h c) -> p i h c", i=TT, h=2)
        yT = proj_q
        out_rows = raw_flat.rearrange("p (i c) -> p i c", i=TT)
        g_final = ff_gate[:, :, :].rearrange("p a b -> p (a b)")

        b_tile = vecs[:, 0:PROJ_TILES]
        g_mix = vecs[:, 32:32 + KT]
        g_ffn = vecs[:, 32 + KT:32 + 2 * KT]
        pos = [vecs[:, 64 + CMP_LEN * s:64 + CMP_LEN * (s + 1)] for s in range(2)]

        consts_in = sem("consts_in")
        rel_in = sem("rel_in")
        rel_read = sem("rel_read")
        setup_pool = sem("setup_pool")
        ident_made = sem("ident_made")
        valid_made = sem("valid_made")
        ones_made = sem("ones_made")
        setup_pe = sem("setup_pe")
        vecs_ready = sem("vecs_ready")
        bias_built = sem("bias_built")
        bias_saved = sem("bias_saved")
        x_in = [sem(f"x_in{s}") for s in range(2)]
        xT_ready = sem("xT_ready")
        x_staged = sem("x_staged")
        x_saved = [sem(f"x_saved{s}") for s in range(2)]
        xg_staged = sem("xg_staged")
        act_hi_done = sem("act_hi_done")
        act_lo_done = sem("act_lo_done")
        squared = sem("squared")
        square_added = sem("square_added")
        sum_ready = sem("sum_ready")
        mean_ready = sem("mean_ready")
        root_ready = sem("root_ready")
        raw_in = [sem(f"raw_in{s}") for s in range(RAW)]
        hi_done = sem("hi_done")
        lo_done = sem("lo_done")
        unit_done = sem("unit_done")
        bank_read = sem("bank_read")
        biased = sem("biased")
        dve_chain = sem("dve_chain")
        w1_in = [sem(f"w1_in{s}") for s in range(2)]
        gate_exp = sem("gate_exp")
        gate_made = sem("gate_made")
        prep_pe = sem("prep_pe")
        blocks_made = sem("blocks_made")
        gelu_done = sem("gelu_done")
        v_copied = sem("v_copied")
        hid_copied = sem("hid_copied")
        kc_made = sem("kc_made")
        prep_done = sem("prep_done")
        table_in = [sem(f"table_in{s}") for s in range(4)]
        stack_hi = sem("stack_hi")
        stack_lo = sem("stack_lo")
        scored = sem("scored")
        masked = sem("masked")
        exped = sem("exped")
        normed = sem("normed")
        transposed = sem("transposed")
        copied = sem("copied")
        pv_done = sem("pv_done")
        o_hi = sem("o_hi")
        o_lo = sem("o_lo")
        y_in = sem("y_in")
        gate_silu = sem("gate_silu")
        gate_ready = sem("gate_ready")
        ff_staged = sem("ff_staged")
        ff_hi_done = sem("ff_hi_done")
        ff_lo_done = sem("ff_lo_done")
        g_final_in = sem("g_final_in")
        out_transposed = sem("out_transposed")
        out_squared = sem("out_squared")
        out_copied = sem("out_copied")
        out_root = sem("out_root")
        out_scaled = sem("out_scaled")
        out_saved = sem("out_saved")

        ALL_READ = tiles_before(IN_GROUPS)
        CONSTS = 14
        OUT_READ = tiles_before(FF_GROUP0)

        def stack_sources(r):
            slot = r % 2
            group_b = 4 * r >= NSA_HEADS
            q0 = (Q_B + 2 * (r - ROUNDS // 2)) if group_b else Q_A + 2 * r
            his, los = [], []
            for o in range(4):
                f = 64 * (o % 2)
                src = tile_of(q0 + o // 2)[f:f + 64, :]
                stack = w_hi[:, slot, SEQ * o:SEQ * (o + 1)]
                his.append((src, stack[f:f + 64, :], -SCALE))
                los.append((len(his), src, stack[f:f + 64, :], stack[64 - f:128 - f, :], -SCALE))
            kv = (r - ROUNDS // 2) // 2 if group_b else r
            f = 64 * (kv % 2)
            for n, t in enumerate([K_B] if group_b else [K_S + kv // 2, K_W + kv // 2]):
                src = tile_of(t)[f:f + 64, :]
                k_hi = w_lo[:, slot, 2 * SEQ * n:2 * SEQ * n + SEQ]
                k_lo = w_lo[:, slot, 2 * SEQ * n + SEQ:2 * SEQ * (n + 1)]
                for d in (0, 64):
                    his.append((src, k_hi[d:d + 64, :], 1.0))
                for d in (0, 64):
                    los.append((len(his), src, k_hi[f:f + 64, :], k_lo[d:d + 64, :], 1.0))
            return his, los
        READ_PER_BLOCK = 4 * 5

        def unit_at(step):
            if step < N_IN:
                return IN_UNITS[step][2], IN_UNITS[step][4]
            return UNIT_KT, UNIT_COLS

        def raw_unit(slot, kt=UNIT_KT, cols=UNIT_COLS):
            return raw[:, slot, :].rearrange("p (t c) -> p t c", t=kt)

        def rows(w, r0, kt, c0, cols):
            return w[bass.ds(r0, kt * P), bass.ds(c0, cols)].rearrange("(t p) c -> p t c", p=P)

        block = ctx.enter_context(nc.Block())

        @block.sync
        def _(sp):
            def load(src, step, i=0, per=0, kt=UNIT_KT):
                slot = step % RAW
                if step >= RAW:
                    sp.wait_ge(lo_done, step - RAW + 1 + per * i)
                sp.dma_start(raw_unit(slot, kt), src).then_inc(raw_in[slot], 16)

            def load_in(step):
                _, k, kt, c0, n, _ = IN_UNITS[step]
                load(rows(w_in, P * k, kt, c0, n), step, kt=kt)

            def load_x(c):
                if c >= 2:
                    sp.wait_ge(xT_ready, 4 * (c - 1))
                sp.dma_start(x_chunk[c % 2], x[:, UNIT_COLS * c:UNIT_COLS * (c + 1)].rearrange(
                    "(i p) c -> p i c", p=P)).then_inc(x_in[c % 2], 16)

            load_x(0)
            sp.dma_start(vec_rows[32:32 + KT, :], norm_mix[0].rearrange("(r c) -> r c", c=P))\
              .then_inc(consts_in, 16)
            sp.dma_start(vec_rows[48:48 + KT, :], norm_ffn[0].rearrange("(r c) -> r c", c=P))\
              .then_inc(consts_in, 16)
            for c0, n, tile in IN_RUNS:
                if tile in (Q_A + 4, Q_B + 4):
                    continue
                n = 2 * n if tile in (Q_A, Q_B) else n
                sp.dma_start(vec_rows[tile:tile + n // P, :],
                             b_in[c0:c0 + n].rearrange("(r c) -> r c", c=P)).then_inc(consts_in, 16)
            sp.dma_start(vec_rows[PROJ_TILES:32, :], b_in[0:P].rearrange("(r c) -> r c", c=P))\
              .then_inc(consts_in, 16)
            for s, p in enumerate((cmp_pos_k[0], cmp_pos_v[0])):
                for half in range(2):
                    sp.dma_start(vec_rows[64 + 32 * s:96 + 32 * s, 64 * half:64 * half + 64], p)\
                      .then_inc(consts_in, 16)
            load_in(0)
            load_x(1)
            sp.dma_start(rel_rows, rel_bias).then_inc(rel_in, 16)
            sp.dma_start(sink_sb[:, 0, :], bass.AP(sinks.tensor, sinks.offset, [[0, P], [1, SWA_HEADS]]))\
              .then_inc(rel_in, 16)
            for half in range(2):
                sp.dma_start(w2k[:, :, half, :], cmp_k_w2[0].rearrange("(k p) d -> p k d", p=P))\
                  .then_inc(rel_in, 16)
            sp.dma_start(w2v[:, :, :], cmp_v_w2[0].rearrange("(k p) d -> p k d", p=P))\
              .then_inc(rel_in, 16)
            load_in(1)
            load_in(2)
            load_x(2)
            load_in(3)
            load_x(3)
            sp.wait_ge(bias_built, 2)
            for h0, n in ((0, NSA_HEADS), (NSA_HEADS, SWA_HEADS)):
                off = 0 if h0 == 0 else BIAS_W
                src = bias_rows[h0:h0 + n, off:off + BIAS_W]
                sp.dma_start(bias_dram.ap()[h0:h0 + n, :, :],
                             bass.AP(src.tensor, src.offset,
                                     [list(src.ap[0]), [0, P], [1, BIAS_W]]))\
                  .then_inc(bias_saved, 16)
            for step in range(4, N_IN):
                load_in(step)

            sp.wait_ge(lo_done, N_IN)
            for s, w in enumerate((cmp_k_w1[0], cmp_v_w1[0])):
                sp.dma_start(w1[s], w.rearrange("(j p) m -> p j m", p=P)).then_inc(w1_in[s], 16)

            def load_table(h):
                if h >= 4:
                    sp.wait_ge(masked, 4 * (last_item(h - 4) + 1))
                first = 0 if h < NSA_HEADS else 2 * P
                sp.dma_start(tables[:, h % 4, first:SEQ],
                             bass.AP(bias_dram, h * P * BIAS_W + P - 1 + first,
                                     [[BIAS_W - 1, P], [1, SEQ - first]])).then_inc(table_in[h % 4], 16)

            sp.wait_ge(bias_saved, 32)
            sp.wait_ge(prep_pe, PREP["hidden1"])
            for h in range(HEADS):
                load_table(h)
                if h == HEADS - 4:
                    sp.wait_ge(stack_lo, STACK_BEFORE[ROUNDS])
                    sp.wait_ge(x_saved[0], 16 * KT // 2)
                    sp.wait_ge(x_saved[1], 16 * KT // 2)
                    sp.dma_start(yT[:, :, :], xT_dram.rearrange("k p c -> p k c"))\
                      .then_inc(y_in, 16)

            sp.wait_ge(pv_done, len(PV_RUNS))
            for q in range(4):
                for k in range(4):
                    load(rows(w_out, UNIT_COLS * k, UNIT_KT, UNIT_COLS * q, UNIT_COLS),
                         OUT0 + 4 * q + k)
            for j in range(8):
                w = w_gate if j < 4 else w_up
                load(rows(w, UNIT_COLS * (j % 4), UNIT_KT, 0, UNIT_COLS), FF0 + j)
            with sp.Fori(0, FF_BLOCKS - 1) as i:
                for j in range(PER_BLOCK):
                    w = (w_gate, w_down, w_up)[j // 4]
                    if j // 4 == 1:
                        src = rows(w, i * UNIT_COLS, UNIT_KT, UNIT_COLS * (j % 4), UNIT_COLS)
                    else:
                        src = rows(w, UNIT_COLS * (j % 4), UNIT_KT, i * UNIT_COLS + UNIT_COLS,
                                   UNIT_COLS)
                    load(src, LOOP0 + j, i, PER_BLOCK)
            for j in range(4):
                load(rows(w_down, UNIT_COLS * (FF_BLOCKS - 1), UNIT_KT, UNIT_COLS * j, UNIT_COLS),
                     TAIL0 + j)
            sp.wait_ge(ff_staged, 4 * FF_BLOCKS)
            sp.dma_start(g_final, bass.AP(norm_final.tensor, norm_final.offset,
                                          [[0, P], [1, D_MODEL]])).then_inc(g_final_in, 16)
            for i in range(TT):
                sp.wait_ge(out_scaled, i + 1)
                sp.dma_start(out[P * i:P * (i + 1), :], out_rows[:, i, :]).then_inc(out_saved, 16)
            sp.wait_ge(out_saved, 16 * TT)

        @block.gpsimd
        def _(pool):
            nc.gpsimd.memset(ident[:, :], 0.0).then_inc(setup_pool, 1)
            nc.gpsimd.memset(valid[:, :], 1.0).then_inc(setup_pool, 1)
            pool.wait_ge(setup_pool, 2)
            nc.gpsimd.affine_select(out=ident[:, :], in_=ident[:, :], compare_op=ALU.not_equal,
                                    fill=1.0, base=0, pattern=[[-1, P]], channel_multiplier=1)\
              .then_inc(ident_made, 1)
            nc.gpsimd.affine_select(out=valid[:, :], in_=valid[:, :], compare_op=ALU.is_ge,
                                    fill=0.0, base=-(CMP_LEN - 1), pattern=[[0, 1]],
                                    channel_multiplier=1).then_inc(valid_made, 1)
            for k in range(KT):
                pool.wait_ge(x_staged, k + 1)
                if k >= 2:
                    pool.wait_ge(square_added, k - 1)
                nc.gpsimd.tensor_tensor(square[k % 2], x_stage[k % 2], x_stage[k % 2], ALU.mult)\
                  .then_inc(squared, 1)

            def scale_gate(base, i=0):
                for t in range(4):
                    pool.wait_ge(gate_silu, base + t + 1 + i * 4)
                    nc.gpsimd.tensor_tensor(ff_gate[:, t, :], ff_gate[:, t, :], rstd, ALU.mult)\
                      .then_inc(gate_ready, 1)

            scale_gate(0)
            with pool.Fori(0, FF_BLOCKS - 1) as i:
                scale_gate(4, i)

        @block.scalar
        def _(act):
            def split_hi(step, i=0, per=0):
                kt, cols = unit_at(step)
                act.wait_ge(raw_in[step % RAW], 16 * (step // RAW + 1) + 16 * (per // RAW) * i)
                if step >= RING:
                    act.wait_ge(unit_done, step - RING + 1 + per * i)
                nc.scalar.activation(w_hi[:, step % RING, 0:kt * cols],
                                     raw[:, step % RAW, 0:kt * cols], ACT.Copy)\
                  .then_inc(hi_done, 1)

            def input_tiles(c):
                for k in range(4 * c, 4 * c + 4):
                    ps = SETS[1][k % 4]
                    act.wait_ge(xT_ready, k + 1)
                    if k >= 2:
                        act.wait_ge(x_saved[k % 2], 16 * (k // 2))
                        act.wait_ge(squared, k - 1)
                    nc.scalar.activation(x_stage[k % 2], ps[:, :], ACT.Copy).then_inc(x_staged, 1)
                    if k >= 2:
                        act.wait_ge(act_lo_done, k - 1)
                    if k == 0:
                        act.wait_ge(vecs_ready, 1)
                    nc.scalar.activation(xg_stage[k % 2], ps[:, :], ACT.Copy,
                                         scale=g_mix[:, k:k + 1]).then_inc(xg_staged, 1)
                    act.wait_ge(x_staged, k + 1)
                    act.dma_start(xT_dram[k], x_stage[k % 2]).then_inc(x_saved[k % 2], 16)
                    act.wait_ge(xg_staged, k + 1)
                    nc.scalar.activation(act_hi[:, k, :], xg_stage[k % 2], ACT.Copy)\
                      .then_inc(act_hi_done, 1)

            def root(n):
                act.wait_ge(mean_ready, n)
                nc.scalar.activation(square[0], sumsq, ACT.Sqrt).then_inc(root_ready, 1)

            def add_bias(g):
                for t in range(IN_TILES[g]):
                    n = tiles_before(g) + t + 1
                    act.wait_ge(bank_read, n)
                    p = tile_of(IN_RUNS[g][2] + t)
                    nc.scalar.activation(p, p, ACT.Identity,
                                         bias=b_tile[:, IN_RUNS[g][2] + t:IN_RUNS[g][2] + t + 1])\
                      .then_inc(biased, 1)

            for c in range(4):
                input_tiles(c)
                split_hi(c)
            split_hi(4)
            root(1)
            for step in range(5, N_IN + 2):
                if step < N_IN:
                    split_hi(step)
                if step - 2 in IN_LAST:
                    add_bias(IN_LAST.index(step - 2))

            act.wait_ge(biased, ALL_READ)
            g_rows = tile_of(GATE)[0:N_GATES, :]
            nc.scalar.activation(g_rows, g_rows, ACT.Exp, scale=-1.0).then_inc(gate_exp, 1)
            for s in range(2):
                act.wait_ge(prep_pe, PREP[f"hidden{s}"])
                nc.scalar.activation(hidden[s], banks[s][0:ROWS_C, 0:CMP_HIDDEN],
                                     ACT.Gelu_apprx_tanh).then_inc(gelu_done, 1)

            def stack_hi_of(r):
                slot = r % 2
                if r >= 2:
                    act.wait_ge(scored, 4 * first_item(r - 1))
                for src, dst, scale in stack_sources(r)[0]:
                    nc.scalar.activation(dst, src, ACT.Copy, scale=scale).then_inc(stack_hi, 1)

            def exps(x):
                kind, h = ITEMS[x]
                if kind == "c":
                    act.wait_ge(masked, 4 * x + 4)
                    p = prob_c[:, :, h % 4:h % 4 + 2, :]
                    nc.scalar.activation(p, p, ACT.Exp).then_inc(exped, 1)
                    return
                n = HEAD_INDEX[x]
                for i in range(TT):
                    act.wait_ge(masked, 4 * x + i + 1)
                    off, keys = key_columns(kind, i)
                    p = prob[n % 2][:, off:off + P * len(keys)]
                    nc.scalar.activation(p, p, ACT.Exp, scale=-1.0, bias=stats[:, n % 4, 0, i:i + 1],
                                         accum_out=stats[:, n % 4, 1, i:i + 1]).then_inc(exped, 1)
                if kind == "b":
                    nc.scalar.activation(stats[:, n % 4, 2, :], stats[:, n % 4, 0, :], ACT.Exp,
                                         bias=sink_sb[:, 0, h - NSA_HEADS:h - NSA_HEADS + 1])\
                      .then_inc(exped, 1)

            def copies(x):
                kind, _ = ITEMS[x]
                act.wait_ge(transposed, x + 1)
                if kind == "c":
                    if x >= 5:
                        act.wait_ge(pv_done, PV_BEFORE[x - 5] + 1)
                    nc.scalar.activation(pcT, banks[4][:, :], ACT.Copy).then_inc(copied, 1)
                    return
                n = HEAD_INDEX[x]
                if n >= 4:
                    act.wait_ge(pv_done, PV_BEFORE[ITEM_OF[(n - 4) | 1]] + 1)
                for b, dst, cols in T_COPIES["b" if kind == "b" else "n"]:
                    nc.scalar.activation(pT[n % 4][:, dst:dst + cols], banks[4 + b][:, 0:cols],
                                         ACT.Copy).then_inc(copied, 1)

            def out_hi(x):
                m = OUT_AFTER.index(x)
                act.wait_ge(pv_done, PV_BEFORE[x] + 1)
                nc.scalar.activation(act_hi[:, ITEMS[x][1] // 2, :], banks[7][:, :], ACT.Copy)\
                  .then_inc(o_hi, 1)

            act.wait_ge(unit_done, N_IN)
            stack_hi_of(0)
            next_round = 1
            for x in range(N_ITEMS + 2):
                if x < N_ITEMS:
                    exps(x)
                    if next_round < ROUNDS and x == first_item(next_round - 1) + 2:
                        stack_hi_of(next_round)
                        next_round += 1
                if 1 <= x <= N_ITEMS:
                    copies(x - 1)
                if x - 2 in OUT_AFTER:
                    out_hi(x - 2)

            act.wait_ge(scored, 4 * N_ITEMS)
            for step in range(OUT0, OUT0 + N_OUT + 2):
                if step < OUT0 + N_OUT:
                    split_hi(step)
                if step >= OUT0 + 5 and (step - 2 - OUT0) % 4 == 3:
                    q = (step - 2 - OUT0) // 4
                    for c in range(4 * q, 4 * q + 4):
                        act.wait_ge(bank_read, ALL_READ + c + 1)
                        if c >= 2:
                            act.wait_ge(square_added, KT + c - 1)
                        nc.scalar.activation(square[c % 2], yT[:, c, :], ACT.Square)\
                          .then_inc(squared, 1)

            def residual_tiles(c):
                for k in range(4 * c, 4 * c + 4):
                    if k >= 2:
                        act.wait_ge(act_lo_done, KT + k - 1)
                    nc.scalar.activation(ff_stage[:, k % 2, :], yT[:, k, :], ACT.Copy,
                                         scale=g_ffn[:, k:k + 1]).then_inc(xg_staged, 1)
                    act.wait_ge(xg_staged, KT + k + 1)
                    nc.scalar.activation(act_hi[:, k, :], ff_stage[:, k % 2, :], ACT.Copy)\
                      .then_inc(act_hi_done, 1)

            def silu(base, i=0):
                for t in range(4):
                    act.wait_ge(bank_read, base + t + 1 + i * READ_PER_BLOCK)
                    nc.scalar.activation(ff_gate[:, t, :], ff_gate[:, t, :], ACT.Silu)\
                      .then_inc(gate_silu, 1)

            def ff_hi_of(base, i=0):
                for t in range(4):
                    act.wait_ge(ff_staged, base + t + 1 + i * 4)
                    nc.scalar.activation(ff_hi[:, t, :], ff_stage[:, t % 3, :], ACT.Copy)\
                      .then_inc(ff_hi_done, 1)

            act.wait_ge(unit_done, FF0)
            for c in range(4):
                residual_tiles(c)
                split_hi(FF0 + c)
            split_hi(FF0 + 4)
            root(2)
            split_hi(FF0 + 5)
            silu(OUT_READ)
            split_hi(FF0 + 6)
            split_hi(FF0 + 7)
            with act.Fori(0, FF_BLOCKS - 1) as i:
                for j in range(PER_BLOCK):
                    split_hi(LOOP0 + j, i, PER_BLOCK)
                    if j == 1:
                        ff_hi_of(0, i)
                    if j == 5:
                        silu(OUT_READ + 4, i)
            split_hi(TAIL0)
            split_hi(TAIL0 + 1)
            ff_hi_of(4 * (FF_BLOCKS - 1))
            split_hi(TAIL0 + 2)
            split_hi(TAIL0 + 3)
            for q in range(4):
                for i in range(TT):
                    act.wait_ge(out_transposed, 4 * q + i + 1)
                    if 4 * q + i >= 2:
                        act.wait_ge(out_squared, 4 * q + i - 1)
                    nc.scalar.activation(work[:, 512 * (i % 2):512 * (i % 2) + 512],
                                         SETS[q % 2][i][:, :], ACT.Square,
                                         accum_out=squares_by_row[:, i, q:q + 1])\
                      .then_inc(out_squared, 1)
            act.wait_ge(mean_ready, 3)
            nc.scalar.activation(stats[:, 1, 0, :], stats[:, 0, 0, :], ACT.Sqrt)\
              .then_inc(out_root, 1)

        @block.vector
        def _(dve):
            chain = [0]

            def then(ins):
                chain[0] += 1
                ins.then_inc(dve_chain, 1)
                dve.wait_ge(dve_chain, chain[0])

            def split_lo(step, i=0, per=0):
                kt, cols = unit_at(step)
                dve.wait_ge(hi_done, step + 1 + per * i)
                n = kt * cols
                nc.vector.tensor_tensor(w_lo[:, step % RING, 0:n], raw[:, step % RAW, 0:n],
                                        w_hi[:, step % RING, 0:n].bitcast(F32), ALU.subtract)\
                  .then_inc(lo_done, 1)

            def add_square(k, n):
                dve.wait_ge(squared, n + 1)
                if k == 0:
                    nc.vector.tensor_copy(sumsq, square[n % 2]).then_inc(square_added, 1)
                else:
                    dve.wait_ge(square_added, n)
                    nc.vector.tensor_tensor(sumsq, sumsq, square[n % 2], ALU.add)\
                      .then_inc(square_added, 1)

            def input_tiles(c):
                for k in range(4 * c, 4 * c + 4):
                    dve.wait_ge(act_hi_done, k + 1)
                    nc.vector.tensor_tensor(act_lo[:, k, :], xg_stage[k % 2],
                                            act_hi[:, k, :].bitcast(F32), ALU.subtract)\
                      .then_inc(act_lo_done, 1)
                    add_square(k, k)

            def newton(mean, root_of, y, t):
                then(nc.vector.reciprocal(y, root_of))
                then(nc.vector.tensor_tensor(t, y, y, ALU.mult))
                then(nc.vector.tensor_tensor(t, t, mean, ALU.mult))
                then(nc.vector.tensor_scalar(t, t, -0.5, 1.5, ALU.mult, ALU.add))
                then(nc.vector.tensor_tensor(y, y, t, ALU.mult))

            def mean_square(bank, n):
                dve.wait_ge(sum_ready, n)
                dve.wait_ge(square_added, KT * n)
                nc.vector.tensor_scalar(sumsq, bank[:, :], 1.0 / D_MODEL, RMS_EPS, ALU.mult, ALU.add)\
                  .then_inc(mean_ready, 1)

            def rstd_of(n):
                dve.wait_ge(mean_ready, n)
                dve.wait_ge(root_ready, n)
                newton(sumsq, square[0], rstd, square[1])

            def scale_group(g):
                dve.wait_ge(unit_done, IN_LAST[g] + 1)
                if IN_RUNS[g][2] == K_C:
                    dve.wait_ge(bias_saved, 32)
                if IN_RUNS[g][2] == K_B:
                    for s in range(2):
                        dve.wait_ge(x_saved[s], 16 * KT // 2)
                for t in range(IN_TILES[g]):
                    nc.vector.tensor_tensor(tile_of(IN_RUNS[g][2] + t), SETS[g % 2][t][:, :], rstd,
                                            ALU.mult).then_inc(bank_read, 1)

            nc.vector.memset(ones[:, :], 1.0).then_inc(ones_made, 1)
            nc.vector.memset(kc_hi[:, :, :].bitcast(F32), 0.0).then_inc(ones_made, 1)
            nc.vector.memset(kc_lo[:, :, :].bitcast(F32), 0.0).then_inc(ones_made, 1)
            dve.wait_ge(setup_pe, 1)
            nc.vector.tensor_copy(vecs[:, :], banks[0][:, 0:P]).then_inc(vecs_ready, 1)
            input_tiles(0)
            split_lo(0)
            dve.wait_ge(setup_pe, 2)
            nc.vector.tensor_scalar(rel_t, banks[1][0:HEADS, 0:NUM_BUCKETS], -1.0, None, ALU.mult)\
              .then_inc(rel_read, 1)
            dve.wait_ge(rel_read, 1)
            then(nc.vector.memset(bias_rows[:, 0:2 * BIAS_W], MASKED))
            bucket = bucket_of_distance()
            runs = []
            for b in sorted(set(bucket.tolist())):
                ds = np.flatnonzero(bucket == b)
                runs.append((b, int(ds[0]), int(ds[-1])))
            for b, d0, d1 in runs:
                n = d1 - d0 + 1
                last = nc.vector.tensor_copy(bias_rows[:, SEQ - 1 - d1:SEQ - d0],
                                             rel_t[:, b:b + 1].to_broadcast([HEADS, n]))
            last.then_inc(bias_built, 1)
            for b, d0, d1 in runs:
                d1 = min(d1, SWA_WINDOW - 1)
                if d0 <= d1:
                    n = d1 - d0 + 1
                    last = nc.vector.tensor_copy(
                        bias_rows[:, BIAS_W + SEQ - 1 - d1:BIAS_W + SEQ - d0],
                        rel_t[:, b:b + 1].to_broadcast([HEADS, n]))
            last.then_inc(bias_built, 1)
            dve.wait_ge(rel_in, 16 * 5)
            nc.vector.tensor_scalar(sink_sb[:, 1, :], sink_sb[:, 0, :], -1.0, None, ALU.mult)\
              .then_inc(ones_made, 1)
            for c in range(1, 4):
                input_tiles(c)
                split_lo(c)
            mean_square(SETS[1][0], 1)
            split_lo(4)
            rstd_of(1)
            for step in range(5, N_IN + 2):
                if step < N_IN:
                    split_lo(step)
                if step - 2 in IN_LAST:
                    scale_group(IN_LAST.index(step - 2))

            def make_blocks(s):
                for t in range(2):
                    for half in range(2):
                        src = tile_of((K_C, V_C)[s] + t)[64 * half:64 * half + 64, :]
                        for lp in range(2):
                            for jj in range(2):
                                v = src[:, CMP_STRIDE * jj + lp:]
                                v = bass.AP(src.tensor, v.offset,
                                            [list(src.ap[0]), [2, 8], [CMP_STRIDE, N_CMP]])
                                pv = pos[s][64 * half:64 * half + 64, :]
                                pv = bass.AP(pv.tensor, pv.offset + CMP_STRIDE * jj + lp,
                                             [list(pv.ap[0]), [2, 8], [0, N_CMP]])
                                last = nc.vector.tensor_tensor(
                                    blocks[64 * lp:64 * lp + 64, 8 * jj:8 * jj + 8, 2 * t + half, :],
                                    v, pv, ALU.add)
                last.then_inc(blocks_made, 1)

            dve.wait_ge(biased, ALL_READ)
            make_blocks(0)
            dve.wait_ge(gate_exp, 1)
            g_rows = tile_of(GATE)[0:N_GATES, :]
            then(nc.vector.tensor_scalar(g_rows, g_rows, 1.0, None, ALU.add))
            nc.vector.reciprocal(g_rows, g_rows).then_inc(gate_made, 1)
            for n, t in enumerate((V_S, V_S + 1, V_W, V_W + 1, V_B)):
                dve.wait_ge(prep_pe, PREP[f"v{n}"])
                nc.vector.tensor_copy(tile_of(t), banks[3 + n][:, :]).then_inc(v_copied, 1)
            dve.wait_ge(prep_pe, PREP["hidden0"])
            make_blocks(1)
            dve.wait_ge(prep_pe, PREP["gates"])
            dve.wait_ge(valid_made, 1)
            then(nc.vector.tensor_copy(gates[:, :, :].rearrange("p i g -> p (i g)"),
                                       banks[2][:, 0:TT * N_GATES]))
            g_c = gates[:, 0, :].rearrange("p (h b) -> p h b", b=3)[:, :, 0:1]
            nc.vector.tensor_scalar(g_c, g_c, valid[:, 0:1], None, ALU.mult).then_inc(gate_made, 1)
            dve.wait_ge(prep_pe, PREP["hidT0"])
            nc.vector.tensor_copy(hid_k, banks[0][:, 0:2 * ROWS_C].rearrange(
                "p (k n) -> p k n", k=2)).then_inc(hid_copied, 1)
            dve.wait_ge(prep_pe, PREP["hidden1"])
            then(nc.vector.memset(hid_v, 0.0))
            then(nc.vector.memset(vc_pad, 0.0))
            dve.wait_ge(prep_pe, PREP["hidT1"])
            for k in range(2):
                for r in range(4):
                    last = nc.vector.tensor_copy(
                        hid_v[:, k, :, r, 0:N_CMP],
                        banks[1][:, ROWS_C * k:ROWS_C * (k + 1)].rearrange(
                            "p (h n) -> p h n", h=NSA_KV))
            last.then_inc(hid_copied, 1)
            dve.wait_ge(prep_pe, PREP["kc"])
            dve.wait_ge(ones_made, 4)
            kc_ps = banks[2][:, 0:ROWS_C].rearrange("p (h n) -> p h n", h=NSA_KV)
            then(nc.vector.tensor_copy(kc_hi[:, :, 0:N_CMP], kc_ps))
            nc.vector.tensor_tensor(kc_lo[:, :, 0:N_CMP], kc_ps, kc_hi[:, :, 0:N_CMP].bitcast(F32),
                                    ALU.subtract).then_inc(kc_made, 1)
            dve.wait_ge(prep_pe, PREP["vc"])
            for h in range(4):
                last = nc.vector.tensor_copy(
                    vc_pad[32 * h:32 * h + 32, :, h, :],
                    banks[3][32 * h:32 * h + 32, 0:NSA_KV * HEAD_DIM].rearrange(
                        "p (k d) -> p k d", k=NSA_KV))
            last.then_inc(kc_made, 1)
            then(nc.vector.memset(score_c, MASKED))
            nc.vector.memset(prob_c, 0.0).then_inc(prep_done, 1)

            def stack_lo_of(r):
                if r >= 2:
                    dve.wait_ge(scored, 4 * first_item(r - 1))
                for n, src, hi, dst, scale in stack_sources(r)[1]:
                    dve.wait_ge(stack_hi, STACK_BEFORE[r] + n)
                    nc.vector.scalar_tensor_tensor(dst, src, scale, hi.bitcast(F32), ALU.mult,
                                                   ALU.subtract).then_inc(stack_lo, 1)

            def mask_scores(x):
                kind, h = ITEMS[x]
                if kind == "c":
                    dve.wait_ge(scored, 4 * x + 4)
                    for o in range(2):
                        dve.wait_ge(table_in[(h + o) % 4], 16 * (h // 4 + 1))
                    if x >= 5:
                        dve.wait_ge(transposed, x - 4)
                    ps = banks[0][:, 0:256].rearrange("p (i h c) -> p i h c", i=TT, h=2)
                    for i in range(TT):
                        n = 8 * i + 7
                        tab = tables[:, h % 4:h % 4 + 2, :]
                        tab = bass.AP(tab.tensor, tab.offset + SEQ - P - P * i + CMP_LEN - 1,
                                      [list(tab.ap[0]), [SEQ, 2], [CMP_STRIDE, n]])
                        last = nc.vector.tensor_tensor(score_c[:, i, :, 0:n], ps[:, i, :, 0:n], tab,
                                                       ALU.add)
                        if i < TT - 1:
                            last.then_inc(masked, 1)
                    then(last)
                    least = cstats[:, 0, :].rearrange("p (i h) -> p i h", i=TT)
                    then(nc.vector.tensor_reduce(least, score_c, AX.X, ALU.min))
                    nc.vector.tensor_tensor(
                        prob_c[:, :, h % 4:h % 4 + 2, :],
                        least.unsqueeze(3).to_broadcast([P, TT, 2, 32]), score_c, ALU.subtract)\
                      .then_inc(masked, 1)
                    return
                n = HEAD_INDEX[x]
                if kind != "w":
                    dve.wait_ge(table_in[h % 4], 16 * (h // 4 + 1))
                if n >= 2:
                    dve.wait_ge(transposed, ITEM_OF[n - 2] + 1)
                if n >= 4:
                    dve.wait_ge(normed, NORM_BEFORE[ITEM_OF[n - 4]] + 4)
                for i in range(TT):
                    off, keys = key_columns(kind, i)
                    cols = P * len(keys)
                    dve.wait_ge(scored, 4 * x + i + 1)
                    first = banks[i][:, 0:cols]
                    init = 3e38
                    if kind == "b":
                        init = sink_sb[:, 1, h - NSA_HEADS:h - NSA_HEADS + 1]
                    nc.vector.tensor_tensor_reduce(
                        prob[n % 2][:, off:off + cols], first, tables[:, h % 4, SEQ - cols:SEQ],
                        1.0, init, ALU.add, ALU.min, stats[:, n % 4, 0, i:i + 1])\
                      .then_inc(masked, 1)

            def normalise(x):
                kind, h = ITEMS[x]
                if kind == "c":
                    p = prob_c[:, :, h % 4:h % 4 + 2, :]
                    dve.wait_ge(exped, EXP_BEFORE[x] + 1)
                    total = cstats[:, 1, :].rearrange("p (i h) -> p i h", i=TT)
                    rec = cstats[:, 2, :].rearrange("p (i h) -> p i h", i=TT)
                    then(nc.vector.tensor_reduce(total, p, AX.X, ALU.add))
                    then(nc.vector.reciprocal(rec, total))
                    g = gates[:, :, 3 * h:3 * h + 6].rearrange("p i (h b) -> p i h b", b=3)[:, :, :, 0]
                    then(nc.vector.tensor_tensor(rec, rec, g, ALU.mult))
                    nc.vector.tensor_tensor(p, p, rec.unsqueeze(3).to_broadcast([P, TT, 2, 32]),
                                            ALU.mult).then_inc(normed, 1)
                    return
                n = HEAD_INDEX[x]
                dve.wait_ge(exped, EXP_BEFORE[x] + (5 if kind == "b" else 4))
                total, rec = stats[:, n % 4, 1, :], stats[:, n % 4, 2, :]
                if kind == "b":
                    then(nc.vector.tensor_tensor(total, total, rec, ALU.add))
                    then(nc.vector.reciprocal(rec, total))
                else:
                    then(nc.vector.reciprocal(rec, total))
                    g = 3 * h + (1 if kind == "s" else 2)
                    then(nc.vector.tensor_tensor(rec, rec, gates[:, :, g], ALU.mult))
                for i in range(TT):
                    off, keys = key_columns(kind, i)
                    p = prob[n % 2][:, off:off + P * len(keys)]
                    nc.vector.tensor_scalar(p, p, rec[:, i:i + 1], None, ALU.mult)\
                      .then_inc(normed, 1)

            def out_lo(x):
                m = OUT_AFTER.index(x)
                dve.wait_ge(o_hi, m + 1)
                t = ITEMS[x][1] // 2
                nc.vector.tensor_tensor(act_lo[:, t, :], banks[7][:, :],
                                        act_hi[:, t, :].bitcast(F32), ALU.subtract)\
                  .then_inc(o_lo, 1)

            dve.wait_ge(kc_made, 2)
            dve.wait_ge(gate_made, 2)
            stack_lo_of(0)
            next_round = 1
            for x in range(N_ITEMS + 2):
                if x < N_ITEMS:
                    mask_scores(x)
                if 1 <= x <= N_ITEMS:
                    normalise(x - 1)
                if x < N_ITEMS and next_round < ROUNDS and x == first_item(next_round - 1) + 2:
                    stack_lo_of(next_round)
                    next_round += 1
                if x - 2 in OUT_AFTER:
                    out_lo(x - 2)

            for step in range(OUT0, OUT0 + N_OUT + 2):
                if step < OUT0 + N_OUT:
                    split_lo(step)
                if step >= OUT0 + 5 and (step - 2 - OUT0) % 4 == 3:
                    q = (step - 2 - OUT0) // 4
                    dve.wait_ge(unit_done, step - 1)
                    dve.wait_ge(y_in, 16)
                    for t in range(4):
                        nc.vector.tensor_tensor(yT[:, 4 * q + t, :], yT[:, 4 * q + t, :],
                                                SETS[(OUT_GROUP0 + q) % 2][t][:, :], ALU.add)\
                          .then_inc(bank_read, 1)
                    for c in range(4 * q, 4 * q + 4):
                        add_square(c, KT + c)

            def residual_tiles(c):
                for k in range(4 * c, 4 * c + 4):
                    dve.wait_ge(act_hi_done, KT + k + 1)
                    nc.vector.tensor_tensor(act_lo[:, k, :], ff_stage[:, k % 2, :],
                                            act_hi[:, k, :].bitcast(F32), ALU.subtract)\
                      .then_inc(act_lo_done, 1)

            def gate_out(group, base_unit, i=0):
                dve.wait_ge(unit_done, base_unit + PER_BLOCK * i)
                for t in range(4):
                    nc.vector.tensor_tensor(ff_gate[:, t, :], SETS[group % 2][t][:, :], rstd, ALU.mult)\
                      .then_inc(bank_read, 1)

            def ff_out(group, base_unit, base, i=0):
                dve.wait_ge(unit_done, base_unit + PER_BLOCK * i)
                for t in range(5):
                    if t < 4:
                        dve.wait_ge(gate_ready, base + t + 1 + i * 4)
                        if t == 3:
                            dve.wait_ge(ff_lo_done, base + 1 + i * 4)
                        nc.vector.tensor_tensor(ff_stage[:, t % 3, :], SETS[group % 2][t][:, :],
                                                ff_gate[:, t, :], ALU.mult).then_inc(ff_staged, 1)
                    if t >= 1:
                        dve.wait_ge(ff_hi_done, base + t + i * 4)
                        nc.vector.tensor_tensor(ff_lo[:, t - 1, :], ff_stage[:, (t - 1) % 3, :],
                                                ff_hi[:, t - 1, :].bitcast(F32), ALU.subtract)\
                          .then_inc(ff_lo_done, 1)

            def down_out(group, base_unit, q, i=0):
                dve.wait_ge(unit_done, base_unit + PER_BLOCK * i)
                for t in range(4):
                    nc.vector.tensor_tensor(yT[:, 4 * q + t, :], yT[:, 4 * q + t, :],
                                            SETS[group % 2][t][:, :], ALU.add)\
                      .then_inc(bank_read, 1)

            for c in range(4):
                residual_tiles(c)
                split_lo(FF0 + c)
            mean_square(SETS[0][0], 2)
            split_lo(FF0 + 4)
            rstd_of(2)
            split_lo(FF0 + 5)
            gate_out(FF_GROUP0, FF0 + 4)
            split_lo(FF0 + 6)
            split_lo(FF0 + 7)
            with dve.Fori(0, FF_BLOCKS - 1) as i:
                for j in range(PER_BLOCK):
                    split_lo(LOOP0 + j, i, PER_BLOCK)
                    done = LOOP0 + j - 1
                    if j == 1:
                        ff_out(LOOP_GROUP0 - 1, done, 0, i)
                    if j == 5:
                        gate_out(LOOP_GROUP0, done, i)
                    if j >= 6 and j < 10:
                        down_out(LOOP_GROUP0 + j - 5, done, j - 6, i)
            split_lo(TAIL0)
            split_lo(TAIL0 + 1)
            ff_out(TAIL_GROUP0 - 1, TAIL0, 4 * (FF_BLOCKS - 1))
            split_lo(TAIL0 + 2)
            down_out(TAIL_GROUP0, TAIL0 + 1, 0)
            split_lo(TAIL0 + 3)
            for q in range(1, 4):
                down_out(TAIL_GROUP0 + q, TAIL0 + q + 1, q)
            dve.wait_ge(g_final_in, 16)
            for q in range(4):
                for i in range(TT):
                    dve.wait_ge(out_squared, 4 * q + i + 1)
                    cols = slice(UNIT_COLS * q, UNIT_COLS * (q + 1))
                    nc.vector.tensor_tensor(out_rows[:, i, cols], SETS[q % 2][i][:, :],
                                            g_final[:, cols], ALU.mult).then_inc(out_copied, 1)
            mean, rows_rstd, t = stats[:, 0, 0, :], stats[:, 0, 1, :], stats[:, 0, 2, :]
            then(nc.vector.tensor_reduce(mean, squares_by_row[:, :, :], AX.X, ALU.add))
            nc.vector.tensor_scalar(mean, mean, 1.0 / D_MODEL, RMS_EPS, ALU.mult, ALU.add)\
              .then_inc(mean_ready, 1)
            dve.wait_ge(mean_ready, 3)
            dve.wait_ge(out_root, 1)
            newton(mean, stats[:, 1, 0, :], rows_rstd, t)
            dve.wait_ge(out_copied, 16)
            for i in range(TT):
                nc.vector.tensor_scalar(out_rows[:, i, :], out_rows[:, i, :], rows_rstd[:, i:i + 1],
                                        None, ALU.mult).then_inc(out_scaled, 1)

        @block.tensor
        def _(pe):
            def unit(step, x_hi, x_lo, dst, first, last, i=0, per=0, kt=UNIT_KT, cols=UNIT_COLS):
                pe.wait_ge(lo_done, step + 1 + per * i)
                wh = w_hi[:, step % RING, 0:kt * cols].rearrange("p (t c) -> p t c", t=kt)
                wl = w_lo[:, step % RING, 0:kt * cols].rearrange("p (t c) -> p t c", t=kt)
                for t in range(kt):
                    for c in range(cols // P):
                        cs = slice(P * c, P * (c + 1))
                        start, stop = first and t == 0, last and t == kt - 1
                        nc.tensor.matmul(dst[c][:, :], wh[:, t, cs], x_lo(t), start=start, stop=False)
                        nc.tensor.matmul(dst[c][:, :], wl[:, t, cs], x_hi(t), start=False, stop=False)
                        done = nc.tensor.matmul(dst[c][:, :], wh[:, t, cs], x_hi(t), start=False,
                                                stop=stop)
                done.then_inc(unit_done, 1)

            def act_unit(step, k0, dst, kt=UNIT_KT, cols=UNIT_COLS, i=0, per=0):
                unit(step, lambda t: act_hi[:, k0 + t, :], lambda t: act_lo[:, k0 + t, :], dst,
                     k0 == 0, k0 + kt == KT, i, per, kt, cols)

            def in_unit(step):
                g, k, kt, _, n, _ = IN_UNITS[step]
                if g == 0:
                    pe.wait_ge(act_lo_done, k + kt)
                if k == 0 and g >= 2:
                    pe.wait_ge(bank_read, tiles_before(g - 1))
                act_unit(step, k, SETS[g % 2], kt, n)

            def transpose_input(c):
                pe.wait_ge(x_in[c % 2], 16 * (c // 2 + 1))
                for k in range(4 * c, 4 * c + 4):
                    if k >= 4:
                        pe.wait_ge(xg_staged, k - 3)
                    for i in range(TT):
                        t = nc.tensor.transpose(SETS[1][k % 4][:, P * i:P * (i + 1)],
                                                x_chunk[c % 2][:, i, P * (k % 4):P * (k % 4 + 1)],
                                                ident[:, :])
                    t.then_inc(xT_ready, 1)

            def sum_squares(bank, n):
                pe.wait_ge(square_added, KT * n)
                nc.tensor.matmul(bank[:, :], ones[:, :], sumsq, start=True, stop=True)\
                  .then_inc(sum_ready, 1)

            pe.wait_ge(ident_made, 1)
            transpose_input(0)
            pe.wait_ge(consts_in, 16 * CONSTS)
            nc.tensor.transpose(banks[0][:, 0:P], vec_rows, ident[:, :]).then_inc(setup_pe, 1)
            pe.wait_ge(rel_in, 16 * 5)
            nc.tensor.transpose(banks[1][0:HEADS, 0:NUM_BUCKETS], rel_rows,
                                ident[0:NUM_BUCKETS, 0:NUM_BUCKETS]).then_inc(setup_pe, 1)
            transpose_input(1)
            pe.wait_ge(vecs_ready, 1)
            pe.wait_ge(rel_read, 1)
            in_unit(0)
            transpose_input(2)
            in_unit(1)
            transpose_input(3)
            in_unit(2)
            pe.wait_ge(ones_made, 1)
            pe.wait_ge(xg_staged, KT)
            sum_squares(SETS[1][0], 1)
            in_unit(3)
            pe.wait_ge(mean_ready, 1)
            for step in range(4, N_IN):
                in_unit(step)

            pe.wait_ge(biased, ALL_READ)
            for n, t in enumerate((V_S, V_S + 1, V_W, V_W + 1, V_B)):
                for j in range(TT):
                    last = nc.tensor.transpose(banks[3 + n][:, P * j:P * (j + 1)],
                                               tile_of(t)[:, P * j:P * (j + 1)], ident[:, :])
                last.then_inc(prep_pe, 1)
            pe.wait_ge(gate_made, 1)
            for j in range(TT):
                last = nc.tensor.transpose(banks[2][:, N_GATES * j:N_GATES * (j + 1)],
                                           tile_of(GATE)[0:N_GATES, P * j:P * (j + 1)],
                                           ident[0:N_GATES, 0:N_GATES])
            last.then_inc(prep_pe, 1)
            for s in range(2):
                pe.wait_ge(w1_in[s], 16)
                pe.wait_ge(blocks_made, s + 1)
                for j in range(16):
                    last = nc.tensor.matmul(banks[s][0:ROWS_C, 0:CMP_HIDDEN],
                                            blocks[:, j, :, :].rearrange("p h n -> p (h n)"),
                                            w1[s][:, j, :], start=j == 0, stop=j == 15)
                last.then_inc(prep_pe, 1)
            for s in range(2):
                pe.wait_ge(gelu_done, s + 1)
                for k in range(2):
                    last = nc.tensor.transpose(banks[s][:, ROWS_C * k:ROWS_C * (k + 1)],
                                               hidden[s][:, P * k:P * (k + 1)],
                                               ident[0:ROWS_C, 0:ROWS_C])
                last.then_inc(prep_pe, 1)
            pe.wait_ge(hid_copied, 1)
            pe.wait_ge(gate_made, 2)
            pe.wait_ge(rel_in, 16 * 5)
            for k in range(2):
                last = nc.tensor.matmul(banks[2][:, 0:ROWS_C],
                                        w2k[:, k, :, :].rearrange("p r d -> p (r d)"),
                                        hid_k[:, k, :], start=k == 0, stop=k == 1)
            last.then_inc(prep_pe, 1)
            pe.wait_ge(hid_copied, 2)
            pe.wait_ge(v_copied, 1)
            for h in range(NSA_KV):
                for k in range(2):
                    last = nc.tensor.matmul(banks[3][:, HEAD_DIM * h:HEAD_DIM * (h + 1)],
                                            hid_v[:, k, h, :, :].rearrange("p r c -> p (r c)"),
                                            w2v[:, k, :], start=k == 0, stop=k == 1)
            last.then_inc(prep_pe, 1)

            def score(x):
                kind, h = ITEMS[x]
                slot, o = h // 4 % 2, h % 4
                if x == first_item(h // 4):
                    pe.wait_ge(stack_lo, STACK_BEFORE[h // 4 + 1])

                def queries(head, i):
                    at = SEQ * (head % 4) + P * i
                    return w_hi[:, slot, at:at + P]

                if kind == "c":
                    if x >= 1:
                        pe.wait_ge(masked, 4 * (x - 1) + 1)
                    for i in range(TT):
                        for e in range(2):
                            at = 64 * i + 32 * e
                            nc.tensor.matmul(banks[0][:, at:at + 32], queries(h + e, i),
                                             kc_lo[:, h // 4, :], start=True, stop=False)
                            last = nc.tensor.matmul(banks[0][:, at:at + 32], queries(h + e, i),
                                                    kc_hi[:, h // 4, :], start=False, stop=True)
                        last.then_inc(scored, 1)
                    return
                k_hi = 2 * SEQ if kind == "w" else 0
                for i in range(TT):
                    if ITEMS[x - 1][0] != "c":
                        pe.wait_ge(masked, 4 * (x - 1) + i + 1)
                    elif i == 0:
                        pe.wait_ge(masked, 4 * x)
                    elif x >= 2:
                        pe.wait_ge(masked, 4 * (x - 2) + i + 1)
                    k0 = max(0, P * (i - 1)) if kind == "b" else 0
                    n = 2 * P if kind == "b" else max(2 * P, P * (i + 1))
                    for at in (k_hi + SEQ, k_hi):
                        last = nc.tensor.matmul(banks[i][:, 0:n], queries(h, i),
                                                w_lo[:, slot, at + k0:at + k0 + n],
                                                start=at != k_hi, stop=at == k_hi)
                    last.then_inc(scored, 1)

            def transpose_probs(x):
                kind, h = ITEMS[x]
                pe.wait_ge(copied, COPY_BEFORE[x])
                if kind == "c":
                    pe.wait_ge(normed, NORM_BEFORE[x] + 1)
                    for i in range(TT):
                        last = nc.tensor.transpose(
                            banks[4][:, P * i:P * (i + 1)],
                            prob_c[:, i, :, :].rearrange("p h c -> p (h c)"), ident[:, :])
                    last.then_inc(transposed, 1)
                    return
                n = HEAD_INDEX[x]
                where = T_BANK["b" if kind == "b" else "n"]
                for i in range(TT):
                    pe.wait_ge(normed, NORM_BEFORE[x] + i + 1)
                    off, keys = key_columns(kind, i)
                    for m, j in enumerate(keys):
                        b, col = where[j]
                        col += P * (i - j)
                        last = nc.tensor.transpose(banks[4 + b][:, col:col + P],
                                                   prob[n % 2][:, off + P * m:off + P * (m + 1)],
                                                   ident[:, :])
                last.then_inc(transposed, 1)

            def products(x):
                kind, h = ITEMS[x]
                h -= h % 2
                pe.wait_ge(copied, COPY_BEFORE[x + 1])
                if kind in "cb":
                    pe.wait_ge(o_lo, sum(y < x for y in OUT_AFTER))
                if kind == "c":
                    for e in range(2):
                        last = nc.tensor.matmul(banks[7][64 * e:64 * e + 64, :],
                                                vc_pad[:, h // 4, h % 4 + e, :], pcT, start=True,
                                                stop=False, skip_group_check=True)
                    last.then_inc(pv_done, 1)
                    return
                n = HEAD_INDEX[x]
                kv = (h - NSA_HEADS) // 8 if kind == "b" else h // 4
                v = tile_of({"s": V_S, "w": V_W, "b": V_B}[kind] + (0 if kind == "b" else kv // 2))
                for j in range(TT):
                    cols = min(2 * P, SEQ - P * j) if kind == "b" else SEQ - P * j
                    at = T_SBUF["b" if kind == "b" else "n"][j]
                    for e in range(2):
                        slot = (n - 1 + e) % 4
                        vcol = P * j + 64 * (kv % 2)
                        last = nc.tensor.matmul(
                            banks[7][64 * e:64 * e + 64, P * j:P * j + cols],
                            v[:, vcol:vcol + 64], pT[slot][:, at:at + cols],
                            start=kind == "b" and j == 0, stop=kind != "s" and j == TT - 1,
                            skip_group_check=True)
                last.then_inc(pv_done, 1)

            pe.wait_ge(kc_made, 2)
            pe.wait_ge(prep_done, 1)
            pe.wait_ge(v_copied, 5)
            for x in range(N_ITEMS + 2):
                if x < N_ITEMS:
                    score(x)
                if 1 <= x <= N_ITEMS:
                    transpose_probs(x - 1)
                if x - 2 in PV_RUNS:
                    products(x - 2)

            pe.wait_ge(o_lo, len(OUT_AFTER))
            for q in range(4):
                g = OUT_GROUP0 + q
                if q >= 2:
                    pe.wait_ge(bank_read, tiles_before(g - 1))
                for k in range(4):
                    act_unit(OUT0 + 4 * q + k, 4 * k, SETS[g % 2])

            pe.wait_ge(bank_read, tiles_before(FF_GROUP0 - 1))
            for k in range(4):
                pe.wait_ge(act_lo_done, KT + 4 * k + 4)
                act_unit(FF0 + k, 4 * k, SETS[FF_GROUP0 % 2])
                if k == 2:
                    pe.wait_ge(bank_read, OUT_READ)
                    sum_squares(SETS[(FF_GROUP0 + 1) % 2][0], 2)
            pe.wait_ge(mean_ready, 2)
            for k in range(4):
                act_unit(FF0 + 4 + k, 4 * k, SETS[(FF_GROUP0 + 1) % 2])

            def down(step, group, i=0, per=0):
                unit(step, lambda t: ff_hi[:, t, :], lambda t: ff_lo[:, t, :], SETS[group % 2],
                     True, True, i, per)

            read0, read_per = OUT_READ + 4, READ_PER_BLOCK
            with pe.Fori(0, FF_BLOCKS - 1) as i:
                pe.wait_ge(bank_read, read0 + read_per * i)
                for k in range(4):
                    act_unit(LOOP0 + k, 4 * k, SETS[LOOP_GROUP0 % 2], i=i, per=PER_BLOCK)
                pe.wait_ge(ff_lo_done, 4 * i + 4)
                for q in range(4):
                    if q:
                        pe.wait_ge(bank_read, read0 + 4 * q + read_per * i)
                    down(LOOP0 + 4 + q, LOOP_GROUP0 + 1 + q, i, PER_BLOCK)
                pe.wait_ge(bank_read, read0 + 16 + read_per * i)
                for k in range(4):
                    act_unit(LOOP0 + 8 + k, 4 * k, SETS[(LOOP_GROUP0 + 5) % 2], i=i, per=PER_BLOCK)
            read1 = read0 + read_per * (FF_BLOCKS - 1)
            for q in range(4):
                pe.wait_ge(bank_read, read1 + max(0, 4 * (q - 1)))
                if q == 0:
                    pe.wait_ge(ff_lo_done, 4 * FF_BLOCKS)
                down(TAIL0 + q, TAIL_GROUP0 + q)

            for q in range(4):
                pe.wait_ge(bank_read, read1 + 4 * 4)
                if q >= 2:
                    pe.wait_ge(out_copied, 4 * (q - 1))
                for i in range(TT):
                    for c in range(4):
                        last = nc.tensor.transpose(SETS[q % 2][i][:, P * c:P * (c + 1)],
                                                   yT[:, 4 * q + c, P * i:P * (i + 1)], ident[:, :])
                    last.then_inc(out_transposed, 1)


_INS = ["x", "rel_bias", "norm_mix", "norm_ffn", "w_in", "b_in", "cmp_pos_k", "cmp_pos_v",
        "cmp_k_w1", "cmp_k_w2", "cmp_v_w1", "cmp_v_w2", "sinks", "w_out", "w_gate", "w_up",
        "w_down", "norm_final"]


def kernel(**inputs):
    import concourse.bacc as bacc
    from concourse.bass_utils import run_bass_kernel_spmd

    nc = bacc.Bacc("TRN2", target_bir_lowering=False, num_devices=1)
    arrays, args = {}, {}
    for name in _INS:
        a = np.ascontiguousarray(inputs[name])
        arrays[f"in_{name}"] = a
        args[name] = nc.dram_tensor(f"in_{name}", a.shape, mybir.dt.from_np(a.dtype),
                                    kind="ExternalInput").ap()
    shape = inputs["x"].shape
    args["out"] = nc.dram_tensor("out_rows_dram", shape, F32, kind="ExternalOutput").ap()
    build(nc, **args)
    r = run_bass_kernel_spmd(nc, [arrays], core_ids=[0])
    return r.results[0]["out_rows_dram"]
```

```python
import math
from contextlib import ExitStack

import numpy as np

import concourse.bass as bass
from concourse import mybir

F32 = mybir.dt.float32
F32R = mybir.dt.float32r
ALU = mybir.AluOpType
ACT = mybir.ActivationFunctionType
AX = mybir.AxisListType

P = 128
SEQ = 512
D_MODEL = 2048
HEAD_DIM = 64
NSA_HEADS = 16
NSA_KV = 4
SWA_HEADS = 16
HEADS = NSA_HEADS + SWA_HEADS
CMP_LEN = 32
CMP_STRIDE = 16
CMP_HIDDEN = 4 * HEAD_DIM
SWA_WINDOW = 128
NUM_BUCKETS = 32
REL_MAX_DISTANCE = 1024
D_FF = 5632
RMS_EPS = 1e-5
MASKED = 1e30
SCALE = HEAD_DIM ** -0.5

KT = D_MODEL // P
TT = SEQ // P
N_CMP = (SEQ - CMP_LEN) // CMP_STRIDE + 1
UNIT_KT = 4
UNIT_COLS = 512
UNIT = UNIT_KT * UNIT_COLS
RAW = 4
RING = 2
FF_BLOCKS = D_FF // UNIT_COLS

Q_A, Q_B, K_S, V_S, K_W, V_W, K_B, V_B, K_C, V_C, GATE = 0, 8, 16, 18, 20, 22, 24, 25, 26, 28, 30
PROJ_TILES = 31
N_GATES = 3 * NSA_HEADS

IN_RUNS = [(1024, 512, K_C), (1536, 512, K_S), (2048, 512, K_W), (2560, P, GATE), (3632, 256, K_B),
           (0, 512, Q_A), (512, 512, Q_A + 4), (2608, 512, Q_B), (3120, 512, Q_B + 4)]

NSA_COLS = P * TT * (TT + 1) // 2


def bucket_of_distance():
    exact = NUM_BUCKETS // 2
    d = np.arange(SEQ)
    ratio = np.log(np.maximum(d, 1).astype(np.float32) / np.float32(exact)) / np.float32(
        math.log(REL_MAX_DISTANCE / exact))
    large = exact + (ratio * np.float32(NUM_BUCKETS - exact)).astype(np.int32)
    return np.where(d < exact, d, np.minimum(large, NUM_BUCKETS - 1))


def in_units():
    units = []
    for g, (c0, n, tile) in enumerate(IN_RUNS):
        kt = UNIT // n
        units += [(g, k, kt, c0, n, tile) for k in range(0, KT, kt)]
    return units


IN_UNITS = in_units()
N_IN = len(IN_UNITS)
OUT0 = N_IN
N_OUT = 4 * (D_MODEL // UNIT_COLS)
FF0 = OUT0 + N_OUT
LOOP0 = FF0 + 8
PER_BLOCK = 12
LOOPS = FF_BLOCKS - 2
TAIL0 = LOOP0 + PER_BLOCK * LOOPS
IN_GROUPS = len(IN_RUNS)
IN_LAST = [max(n for n, u in enumerate(IN_UNITS) if u[0] == g) for g in range(IN_GROUPS)]
IN_TILES = [n // P for _, n, _ in IN_RUNS]
OUT_GROUP0 = IN_GROUPS + 1
FF_GROUP0 = OUT_GROUP0 + 4
LOOP_GROUP0 = FF_GROUP0 + 2
GROUPS_PER_BLOCK = 6
TAIL_GROUP0 = LOOP_GROUP0 + GROUPS_PER_BLOCK * LOOPS


def tiles_before(group):
    return sum(IN_TILES[:group]) + 4 * max(0, group - OUT_GROUP0)


ITEMS = []
for _pair in range(NSA_HEADS // 2):
    ITEMS += [("c", 2 * _pair)] + [(_b, 2 * _pair + _o) for _b in "sw" for _o in (0, 1)]
for _h in range(NSA_HEADS, HEADS):
    ITEMS += [("b", _h)]
N_ITEMS = len(ITEMS)
ROUNDS = HEADS // 4


def counts(per_item):
    total = [0]
    for item in ITEMS:
        total.append(total[-1] + per_item(item))
    return total


EXP_BEFORE = counts(lambda it: {"c": 1, "b": 5}.get(it[0], 4))
NORM_BEFORE = counts(lambda it: 1 if it[0] == "c" else 3)
COPY_BEFORE = counts(lambda it: 1 if it[0] == "c" else 2)
THIRD_BEFORE = counts(lambda it: it[0] in "sw")
HEAD_INDEX = counts(lambda it: it[0] != "c")
PV_RUNS = [x for x, (kind, h) in enumerate(ITEMS) if kind == "c" or h % 2]
PV_BEFORE = counts(lambda it: 1 if it[0] == "c" or it[1] % 2 else 0)
OUT_AFTER = [x for x, (kind, h) in enumerate(ITEMS) if kind in "wb" and h % 2]


def first_item(round_):
    return next(x for x, (_, h) in enumerate(ITEMS) if h // 4 == round_)


def last_item(head):
    return max(x for x, (kind, h) in enumerate(ITEMS) if h == head or (kind == "c" and h == head))


def key_columns(kind, i):
    if kind == "b":
        return (0, [0]) if i == 0 else (P + 2 * P * (i - 1), [i - 1, i])
    return P * i * (i + 1) // 2, list(range(i + 1))


T_BANK = {"n": [(0, 0), (1, 0), (2, 0), (1, 384)], "b": [(0, 0), (0, 256), (1, 0), (1, 256)]}
T_SBUF = {"n": [0, 512, 1024, 896], "b": [0, 256, 512, 768]}
T_COPIES = {"n": [(0, 0, 512), (1, 512, 512), (2, 1024, 256)], "b": [(0, 0, 512), (1, 512, 384)]}

ITEM_OF = [x for x, (kind, _) in enumerate(ITEMS) if kind != "c"]
STACK_BEFORE = [0]
for _r in range(ROUNDS):
    STACK_BEFORE.append(STACK_BEFORE[-1] + (8 if 4 * _r < NSA_HEADS else 6))

PREP_AFTER = {6: ["hidden0"], 9: ["hidden1"], 10: ["hidT0"], 16: ["hidT1", "kc", "gates"],
              17: ["vc"], 20: ["v0", "v1", "v2", "v3"], 24: ["v4"]}
PREP = {name: n + 1 for n, name in enumerate(sum(PREP_AFTER.values(), []))}
BIAS_W = SEQ + P


def build(nc, x, rel_bias, norm_mix, norm_ffn, w_in, b_in, cmp_pos_k, cmp_pos_v, cmp_k_w1,
          cmp_k_w2, cmp_v_w1, cmp_v_w2, sinks, w_out, w_gate, w_up, w_down, norm_final, out):
    x, out, b_in = x[0], out[0], b_in[0]
    w_in, w_out, w_gate, w_up, w_down = w_in[0], w_out[0], w_gate[0], w_up[0], w_down[0]
    xT_dram = nc.dram_tensor("xT_scratch", [KT, P, SEQ], F32).ap()
    bias_dram = nc.dram_tensor("bias_scratch", [HEADS, P, BIAS_W], F32)

    with ExitStack() as ctx:
        def sb(name, shape, dt=F32):
            return ctx.enter_context(nc.sbuf_tensor(name, shape, dt))

        def sem(name):
            return ctx.enter_context(nc.semaphore(name))

        act_hi = sb("act_hi", [P, KT, SEQ], F32R)
        act_lo = sb("act_lo", [P, KT, SEQ], F32R)
        proj_q = sb("proj_q", [P, K_S, SEQ])
        raw = sb("raw", [P, RAW, UNIT])
        w_hi = sb("w_hi", [P, RING, UNIT], F32R)
        w_lo = sb("w_lo", [P, RING, UNIT], F32R)
        work = sb("work", [P, 2048])
        ident = sb("ident", [P, P])
        ones = sb("ones", [P, P])
        vecs = sb("vecs", [P, P])
        gates = sb("gates", [P, TT, N_GATES])
        kc_hi = sb("kc_hi", [P, NSA_KV, 32], F32R)
        kc_lo = sb("kc_lo", [P, NSA_KV, 32], F32R)
        stats = sb("stats", [P, 4, 3, TT])
        cstats = sb("cstats", [P, 3, 2 * TT])
        prob_x = sb("prob_x", [P, NSA_COLS])
        sink_sb = sb("sink_sb", [P, 2, SWA_HEADS])
        valid = sb("valid", [P, 1])
        squares_by_row = sb("squares_by_row", [P, TT, 4])
        with nc.sbuf_tensor("proj_kv", [P, PROJ_TILES - K_S, SEQ], F32) as proj_kv:
            pass
        ff_hi = sb("ff_hi", [P, UNIT_KT, SEQ], F32R)
        ff_lo = sb("ff_lo", [P, UNIT_KT, SEQ], F32R)
        ff_gate = sb("ff_gate", [P, UNIT_KT, SEQ])
        ff_stage = sb("ff_stage", [P, 3, SEQ])
        banks = [ctx.enter_context(nc.psum_tensor(f"bank{i}", [P, SEQ], F32)) for i in range(8)]
        SETS = [banks[0:4], banks[4:8]]

        def tile_of(t):
            return proj_q[:, t, :] if t < K_S else proj_kv[:, t - K_S, :]

        x_chunk = [proj_kv[:, 4 * s:4 * s + 4, :] for s in range(2)]
        x_stage = [proj_kv[:, 8 + s, :] for s in range(2)]
        xg_stage = [proj_kv[:, 10 + s, :] for s in range(2)]
        bias_rows = prob_x[0:HEADS, :]
        rel_rows = proj_q[0:HEADS, 9, 0:NUM_BUCKETS]
        rel_t = proj_q[0:HEADS, 9, 128:128 + NUM_BUCKETS]
        vec_rows = proj_q[:, 10, 0:P]
        w2k = proj_q[:, Q_A + 7, 0:4 * HEAD_DIM].rearrange("p (k r d) -> p k r d", k=2, r=2)
        w2v = proj_q[:, Q_A + 7, 4 * HEAD_DIM:6 * HEAD_DIM].rearrange("p (k d) -> p k d", k=2)
        square = [work[:, 0:512], work[:, 512:1024]]
        sumsq = work[:, 1024:1536]
        rstd = work[:, 1536:2048]
        raw_flat = raw[:, :, :].rearrange("p a b -> p (a b)")
        w1 = [proj_q[:, 8 * s:8 * s + 8, :].rearrange("p a (j m) -> p (a j) m", m=CMP_HIDDEN)
              for s in range(2)]
        ROWS_C = NSA_KV * N_CMP
        blocks = [x_chunk[s].rearrange("p a b -> p (a b)")[:, 0:16 * ROWS_C].rearrange(
            "p (j h n) -> p j h n", j=16, h=NSA_KV) for s in range(2)]
        hidden = [tile_of(K_C + s)[0:ROWS_C, 0:CMP_HIDDEN] for s in range(2)]
        hid_k = tile_of(K_C)[:, 256:256 + 2 * ROWS_C].rearrange("p (k n) -> p k n", k=2)
        hid_v = proj_kv[:, V_C - K_S:V_C - K_S + 2, :].rearrange(
            "p k (h r c) -> p k h r c", h=NSA_KV, r=4)
        vc_pad = work[:, 0:NSA_KV * 4 * HEAD_DIM].rearrange("p (k h d) -> p k h d", k=NSA_KV, h=4)
        pT = [raw_flat[:, NSA_COLS * s:NSA_COLS * (s + 1)] for s in range(4)]
        tables = raw_flat[:, 5120:7168].rearrange("p (s c) -> p s c", s=4)
        pcT = raw_flat[:, 7168:7680]
        prob_c = raw_flat[:, 7680:8192].rearrange("p (i h c) -> p i h c", i=TT, h=4)
        prob_flat = proj_kv[:, K_C - K_S:PROJ_TILES - K_S, :].rearrange("p a b -> p (a b)")
        prob = [prob_flat[:, NSA_COLS * s:NSA_COLS * (s + 1)] for s in range(2)] + [prob_x[:, :]]
        pT_b = [raw_flat[:, UNIT + 896 * s:UNIT + 896 * (s + 1)] for s in range(4)]
        tables_b = work[:, 0:1024].rearrange("p (s c) -> p s c", s=4)
        score_c = work[:, 1024:1280].rearrange("p (i h c) -> p i h c", i=TT, h=2)
        yT = proj_q
        out_rows = raw_flat.rearrange("p (i c) -> p i c", i=TT)
        g_final = ff_gate[:, :, :].rearrange("p a b -> p (a b)")

        b_tile = vecs[:, 0:PROJ_TILES]
        g_mix = vecs[:, 32:32 + KT]
        g_ffn = vecs[:, 32 + KT:32 + 2 * KT]
        pos = [vecs[:, 64 + CMP_LEN * s:64 + CMP_LEN * (s + 1)] for s in range(2)]

        consts_in = sem("consts_in")
        rel_in = sem("rel_in")
        w2_in = sem("w2_in")
        rel_read = sem("rel_read")
        setup_pool = sem("setup_pool")
        ident_made = sem("ident_made")
        valid_made = sem("valid_made")
        ones_made = sem("ones_made")
        setup_pe = sem("setup_pe")
        vecs_ready = sem("vecs_ready")
        bias_built = sem("bias_built")
        bias_saved = sem("bias_saved")
        x_in = [sem(f"x_in{s}") for s in range(2)]
        xT_ready = sem("xT_ready")
        x_staged = sem("x_staged")
        x_saved = [sem(f"x_saved{s}") for s in range(2)]
        xg_staged = sem("xg_staged")
        act_hi_done = sem("act_hi_done")
        act_lo_done = sem("act_lo_done")
        squared = sem("squared")
        square_added = sem("square_added")
        sum_ready = sem("sum_ready")
        mean_ready = sem("mean_ready")
        root_ready = sem("root_ready")
        raw_in = [sem(f"raw_in{s}") for s in range(RAW)]
        hi_done = sem("hi_done")
        lo_done = sem("lo_done")
        unit_done = sem("unit_done")
        bank_read = sem("bank_read")
        biased = sem("biased")
        dve_chain = sem("dve_chain")
        w1_in = [sem(f"w1_in{s}") for s in range(2)]
        gate_exp = sem("gate_exp")
        gate_made = sem("gate_made")
        prep_pe = sem("prep_pe")
        blocks_made = sem("blocks_made")
        gelu_done = sem("gelu_done")
        v_copied = sem("v_copied")
        hid_copied = sem("hid_copied")
        kc_made = sem("kc_made")
        prep_done = sem("prep_done")
        table_in = [sem(f"table_in{s}") for s in range(4)]
        stack_hi = sem("stack_hi")
        stack_lo = sem("stack_lo")
        scored = sem("scored")
        masked = sem("masked")
        exped = sem("exped")
        normed = sem("normed")
        factor_made = sem("factor_made")
        third_copied = sem("third_copied")
        last_normed = sem("last_normed")
        transposed = sem("transposed")
        copied = sem("copied")
        pv_done = sem("pv_done")
        o_hi = sem("o_hi")
        o_lo = sem("o_lo")
        y_in = sem("y_in")
        gate_silu = sem("gate_silu")
        gate_ready = sem("gate_ready")
        ff_staged = sem("ff_staged")
        ff_hi_done = sem("ff_hi_done")
        ff_lo_done = sem("ff_lo_done")
        g_final_in = sem("g_final_in")
        out_transposed = sem("out_transposed")
        out_squared = sem("out_squared")
        out_copied = sem("out_copied")
        out_root = sem("out_root")
        out_rstd = sem("out_rstd")
        out_scaled = [sem(f"out_scaled{s}") for s in range(2)]
        out_saved = sem("out_saved")

        ALL_READ = tiles_before(IN_GROUPS)
        SPLIT_AT = first_item(ROUNDS - 1) + 1
        RESIDUAL_ORDER = [(k, (ff_hi, ff_lo)) for k in range(4)] + [
            (k % KT, (act_hi, act_lo)) for k in range(4, KT + 4)]
        CONSTS = 14
        COPIES = 8
        BIAS_SAVED = 16 * 2 * (P // COPIES)
        FIRST_B = next(x for x, (kind, _) in enumerate(ITEMS) if kind == "b")
        C_LAST = max(x for x, (kind, _) in enumerate(ITEMS) if kind == "c")
        OUT_READ = tiles_before(FF_GROUP0)

        V_TILES = [(0, V_S, banks[4]), (1, V_S + 1, banks[5]), (2, V_W, banks[6]),
                   (3, V_W + 1, banks[7]), (4, V_B, banks[0])]

        def stack_sources(r):
            slot = (r + 1) % 2
            group_b = 4 * r >= NSA_HEADS
            q0 = (Q_B + 2 * (r - ROUNDS // 2)) if group_b else Q_A + 2 * r
            his, los = [], []
            for o in range(4):
                f = 64 * (o % 2)
                src = tile_of(q0 + o // 2)[f:f + 64, :]
                stack = w_hi[:, slot, SEQ * o:SEQ * (o + 1)]
                his.append((src, stack[f:f + 64, :], -SCALE))
                los.append((len(his), src, stack[f:f + 64, :], stack[64 - f:128 - f, :], -SCALE))
            kv = (r - ROUNDS // 2) // 2 if group_b else r
            f = 64 * (kv % 2)
            for n, t in enumerate([K_B] if group_b else [K_S + kv // 2, K_W + kv // 2]):
                src = tile_of(t)[f:f + 64, :]
                k_hi = w_lo[:, slot, 2 * SEQ * n:2 * SEQ * n + SEQ]
                k_lo = w_lo[:, slot, 2 * SEQ * n + SEQ:2 * SEQ * (n + 1)]
                for d in (0, 64):
                    his.append((src, k_hi[d:d + 64, :], 1.0))
                for d in (0, 64):
                    los.append((len(his), src, k_hi[f:f + 64, :], k_lo[d:d + 64, :], 1.0))
            return his, los
        READ_TAIL = OUT_READ + 4 + 20 * LOOPS
        READ_PER_BLOCK = 4 * 5

        def unit_at(step):
            if step < N_IN:
                return IN_UNITS[step][2], IN_UNITS[step][4]
            return UNIT_KT, UNIT_COLS

        def raw_unit(slot, kt=UNIT_KT, cols=UNIT_COLS):
            return raw[:, slot, :].rearrange("p (t c) -> p t c", t=kt)

        def rows(w, r0, kt, c0, cols):
            return w[bass.ds(r0, kt * P), bass.ds(c0, cols)].rearrange("(t p) c -> p t c", p=P)

        block = ctx.enter_context(nc.Block())

        @block.sync
        def _(sp):
            def load(src, step, i=0, per=0, kt=UNIT_KT):
                slot = step % RAW
                if step >= RAW:
                    sp.wait_ge(lo_done, step - RAW + 1 + per * i)
                sp.dma_start(raw_unit(slot, kt), src).then_inc(raw_in[slot], 16)

            def load_in(step):
                _, k, kt, c0, n, _ = IN_UNITS[step]
                load(rows(w_in, P * k, kt, c0, n), step, kt=kt)

            def load_x(c):
                if c >= 2:
                    sp.wait_ge(xT_ready, 4 * (c - 1))
                sp.dma_start(x_chunk[c % 2], x[:, UNIT_COLS * c:UNIT_COLS * (c + 1)].rearrange(
                    "(i p) c -> p i c", p=P)).then_inc(x_in[c % 2], 16)

            load_x(0)
            load_in(0)
            load_x(1)
            load_in(1)
            load_x(2)
            load_in(2)
            load_x(3)
            load_in(3)
            load_in(4)
            sp.dma_start(w1[0], cmp_k_w1[0].rearrange("(j p) m -> p j m", p=P))\
              .then_inc(w1_in[0], 16)
            load_in(5)
            load_in(6)
            sp.wait_ge(bias_built, 2)
            sp.dma_start(w1[1], cmp_v_w1[0].rearrange("(j p) m -> p j m", p=P))\
              .then_inc(w1_in[1], 16)
            load_in(7)
            for step in range(8, N_IN):
                load_in(step)
                if step == 11:
                    sp.wait_ge(prep_pe, PREP["hidden0"])
                    for half in range(2):
                        sp.dma_start(w2k[:, :, half, :], cmp_k_w2[0].rearrange(
                            "(k p) d -> p k d", p=P)).then_inc(w2_in, 16)
                    sp.dma_start(w2v, cmp_v_w2[0].rearrange("(k p) d -> p k d", p=P))\
                      .then_inc(w2_in, 16)
                if step < 8 + P // COPIES:
                    c = COPIES * (step - 8)
                    for h0, off in ((0, 0), (NSA_HEADS, BIAS_W)):
                        src = bias_rows[h0:h0 + NSA_HEADS, off:off + BIAS_W]
                        sp.dma_start(bias_dram.ap()[h0:h0 + NSA_HEADS, c:c + COPIES, :],
                                     bass.AP(src.tensor, src.offset,
                                             [list(src.ap[0]), [0, COPIES], [1, BIAS_W]]))\
                          .then_inc(bias_saved, 16)

            sp.wait_ge(lo_done, N_IN)

            def load_out(n):
                load(rows(w_out, UNIT_COLS * (n % 4), UNIT_KT, UNIT_COLS * (n // 4), UNIT_COLS),
                     OUT0 + n)

            def load_table(h):
                if h >= 4:
                    sp.wait_ge(masked, 4 * (last_item(h - 4) + 1))
                if h == NSA_HEADS:
                    sp.wait_ge(pv_done, PV_BEFORE[C_LAST] + 1)
                first = 0 if h < NSA_HEADS else 2 * P
                sp.dma_start((tables if h < NSA_HEADS else tables_b)[:, h % 4, :],
                             bass.AP(bias_dram, h * P * BIAS_W + P - 1 + first,
                                     [[BIAS_W - 1, P], [1, SEQ - first]])).then_inc(table_in[h % 4], 16)

            sp.wait_ge(bias_saved, BIAS_SAVED)
            for h in range(HEADS):
                load_table(h)
                if h == NSA_HEADS + 3:
                    sp.wait_ge(pv_done, PV_BEFORE[FIRST_B])
                    load_out(0)
                    load_out(1)
                if h == HEADS - 4:
                    sp.wait_ge(stack_lo, STACK_BEFORE[ROUNDS])
                    sp.wait_ge(x_saved[0], 16 * KT // 2)
                    sp.wait_ge(x_saved[1], 16 * KT // 2)
                    sp.dma_start(yT[:, :, :], xT_dram.rearrange("k p c -> p k c"))\
                      .then_inc(y_in, 16)

            sp.wait_ge(pv_done, len(PV_RUNS))
            for n in range(2, N_OUT):
                load_out(n)
            for j in range(8):
                w = w_gate if j < 4 else w_up
                load(rows(w, UNIT_COLS * (j % 4), UNIT_KT, 0, UNIT_COLS), FF0 + j)
            with sp.Fori(0, LOOPS) as i:
                for j in range(PER_BLOCK):
                    w = (w_gate, w_down, w_up)[j // 4]
                    if j // 4 == 1:
                        src = rows(w, i * UNIT_COLS, UNIT_KT, UNIT_COLS * (j % 4), UNIT_COLS)
                    else:
                        src = rows(w, UNIT_COLS * (j % 4), UNIT_KT, i * UNIT_COLS + UNIT_COLS,
                                   UNIT_COLS)
                    load(src, LOOP0 + j, i, PER_BLOCK)
            for j in range(16):
                last = UNIT_COLS * (FF_BLOCKS - 1)
                if j < 8:
                    src = rows((w_gate, w_up)[j // 4], UNIT_COLS * (j % 4), UNIT_KT, last, UNIT_COLS)
                else:
                    src = rows(w_down, last - UNIT_COLS * (j < 12), UNIT_KT, UNIT_COLS * (j % 4),
                               UNIT_COLS)
                load(src, TAIL0 + j)
            sp.wait_ge(ff_staged, 4 * FF_BLOCKS)
            sp.dma_start(g_final, bass.AP(norm_final.tensor, norm_final.offset,
                                          [[0, P], [1, D_MODEL]])).then_inc(g_final_in, 16)
            for i in (0, 2, 1, 3):
                sp.wait_ge(out_scaled[i // 2], i % 2 + 1)
                sp.dma_start(out[P * i:P * (i + 1), :], out_rows[:, i, :]).then_inc(out_saved, 16)
            sp.wait_ge(out_saved, 16 * TT)

        @block.gpsimd
        def _(pool):
            nc.gpsimd.memset(ident[:, :], 0.0).then_inc(setup_pool, 1)
            nc.gpsimd.memset(valid[:, :], 1.0).then_inc(setup_pool, 1)
            pool.wait_ge(setup_pool, 2)
            nc.gpsimd.affine_select(out=ident[:, :], in_=ident[:, :], compare_op=ALU.not_equal,
                                    fill=1.0, base=0, pattern=[[-1, P]], channel_multiplier=1)\
              .then_inc(ident_made, 1)
            nc.gpsimd.affine_select(out=valid[:, :], in_=valid[:, :], compare_op=ALU.is_ge,
                                    fill=0.0, base=-(CMP_LEN - 1), pattern=[[0, 1]],
                                    channel_multiplier=1).then_inc(valid_made, 1)
            for k in range(KT):
                pool.wait_ge(x_staged, k + 1)
                if k >= 2:
                    pool.wait_ge(square_added, k - 1)
                nc.gpsimd.tensor_tensor(square[k % 2], x_stage[k % 2], x_stage[k % 2], ALU.mult)\
                  .then_inc(squared, 1)

            for x in ITEM_OF:
                n = HEAD_INDEX[x]
                off, keys = key_columns(ITEMS[x][0], TT - 1)
                p = prob[n % 3][:, off:off + P * len(keys)]
                pool.wait_ge(factor_made, n + 1)
                nc.gpsimd.tensor_scalar(p, p, stats[:, n % 4, 2, TT - 1:TT], None, ALU.mult)\
                  .then_inc(last_normed, 1)

            def scale_gate(base, i=0):
                for t in range(4):
                    pool.wait_ge(gate_silu, base + t + 1 + i * 4)
                    nc.gpsimd.tensor_tensor(ff_gate[:, t, :], ff_gate[:, t, :], rstd, ALU.mult)\
                      .then_inc(gate_ready, 1)

            scale_gate(0)
            with pool.Fori(0, LOOPS) as i:
                scale_gate(4, i)
            scale_gate(4 * (FF_BLOCKS - 1))

        @block.scalar
        def _(act):
            def split_hi(step, i=0, per=0):
                kt, cols = unit_at(step)
                act.wait_ge(raw_in[step % RAW], 16 * (step // RAW + 1) + 16 * (per // RAW) * i)
                if step >= RING:
                    act.wait_ge(unit_done, step - RING + 1 + per * i)
                nc.scalar.activation(w_hi[:, step % RING, 0:kt * cols],
                                     raw[:, step % RAW, 0:kt * cols], ACT.Copy)\
                  .then_inc(hi_done, 1)

            def input_tiles(c):
                for k in range(4 * c, 4 * c + 4):
                    ps = SETS[1][k % 4]
                    act.wait_ge(xT_ready, k + 1)
                    if k >= 2:
                        act.wait_ge(x_saved[k % 2], 16 * (k // 2))
                        act.wait_ge(squared, k - 1)
                    nc.scalar.activation(x_stage[k % 2], ps[:, :], ACT.Copy).then_inc(x_staged, 1)
                    if k >= 2:
                        act.wait_ge(act_lo_done, k - 1)
                    if k == 0:
                        act.wait_ge(vecs_ready, 1)
                    nc.scalar.activation(xg_stage[k % 2], ps[:, :], ACT.Copy,
                                         scale=g_mix[:, k:k + 1]).then_inc(xg_staged, 1)
                    act.wait_ge(x_staged, k + 1)
                    act.dma_start(xT_dram[k], x_stage[k % 2]).then_inc(x_saved[k % 2], 16)
                    act.wait_ge(xg_staged, k + 1)
                    nc.scalar.activation(act_hi[:, k, :], xg_stage[k % 2], ACT.Copy)\
                      .then_inc(act_hi_done, 1)

            def root(n):
                act.wait_ge(mean_ready, n)
                nc.scalar.activation(square[0], sumsq, ACT.Sqrt).then_inc(root_ready, 1)

            def add_bias(g):
                for t in range(IN_TILES[g]):
                    n = tiles_before(g) + t + 1
                    act.wait_ge(bank_read, n)
                    p = tile_of(IN_RUNS[g][2] + t)
                    nc.scalar.activation(p, p, ACT.Identity,
                                         bias=b_tile[:, IN_RUNS[g][2] + t:IN_RUNS[g][2] + t + 1])\
                      .then_inc(biased, 1)

            def stack_hi_of(r):
                if r >= 2:
                    act.wait_ge(scored, 4 * first_item(r - 1))
                for src, dst, scale in stack_sources(r)[0]:
                    nc.scalar.activation(dst, src, ACT.Copy, scale=scale).then_inc(stack_hi, 1)

            act.dma_start(vec_rows[32:32 + KT, :], norm_mix[0].rearrange("(r c) -> r c", c=P))\
               .then_inc(consts_in, 16)
            act.dma_start(vec_rows[48:48 + KT, :], norm_ffn[0].rearrange("(r c) -> r c", c=P))\
               .then_inc(consts_in, 16)
            for c0, n, tile in IN_RUNS:
                if tile in (Q_A + 4, Q_B + 4):
                    continue
                n = 2 * n if tile in (Q_A, Q_B) else n
                act.dma_start(vec_rows[tile:tile + n // P, :],
                              b_in[c0:c0 + n].rearrange("(r c) -> r c", c=P)).then_inc(consts_in, 16)
            act.dma_start(vec_rows[PROJ_TILES:32, :], b_in[0:P].rearrange("(r c) -> r c", c=P))\
               .then_inc(consts_in, 16)
            for s, p in enumerate((cmp_pos_k[0], cmp_pos_v[0])):
                for half in range(2):
                    act.dma_start(vec_rows[64 + 32 * s:96 + 32 * s, 64 * half:64 * half + 64], p)\
                       .then_inc(consts_in, 16)
            act.dma_start(rel_rows, rel_bias).then_inc(rel_in, 16)
            act.dma_start(sink_sb[:, 0, :], bass.AP(sinks.tensor, sinks.offset,
                                                    [[0, P], [1, SWA_HEADS]])).then_inc(rel_in, 16)
            for c in range(4):
                input_tiles(c)
                split_hi(c)
            split_hi(4)
            root(1)
            for step in range(5, N_IN + 2):
                if step < N_IN:
                    split_hi(step)
                if step in (8, 11):
                    s = (8, 11).index(step)
                    act.wait_ge(prep_pe, PREP[f"hidden{s}"])
                    nc.scalar.activation(hidden[s], banks[4 * s][0:ROWS_C, 0:CMP_HIDDEN],
                                         ACT.Gelu_apprx_tanh).then_inc(gelu_done, 1)
                if step - 2 in IN_LAST:
                    add_bias(IN_LAST.index(step - 2))
                if step == 15:
                    act.wait_ge(biased, tiles_before(4))
                    g_rows = tile_of(GATE)[0:N_GATES, :]
                    nc.scalar.activation(g_rows, g_rows, ACT.Exp, scale=-1.0).then_inc(gate_exp, 1)
                if step == N_IN:
                    act.wait_ge(unit_done, N_IN - 1)
                    act.wait_ge(lo_done, N_IN - 1)
                    act.wait_ge(biased, tiles_before(6))
                    stack_hi_of(0)

            def exps(x):
                kind, h = ITEMS[x]
                if kind == "c":
                    act.wait_ge(masked, 4 * x + 4)
                    p = prob_c[:, :, h % 4:h % 4 + 2, :]
                    nc.scalar.activation(p, p, ACT.Exp).then_inc(exped, 1)
                    return
                n = HEAD_INDEX[x]
                for i in range(TT):
                    act.wait_ge(masked, 4 * x + i + 1)
                    off, keys = key_columns(kind, i)
                    p = prob[n % 3][:, off:off + P * len(keys)]
                    nc.scalar.activation(p, p, ACT.Exp, scale=-1.0, bias=stats[:, n % 4, 0, i:i + 1],
                                         accum_out=stats[:, n % 4, 1, i:i + 1]).then_inc(exped, 1)
                if kind == "b":
                    nc.scalar.activation(stats[:, n % 4, 2, :], stats[:, n % 4, 0, :], ACT.Exp,
                                         bias=sink_sb[:, 0, h - NSA_HEADS:h - NSA_HEADS + 1])\
                      .then_inc(exped, 1)

            def copies(x):
                kind, _ = ITEMS[x]
                act.wait_ge(transposed, x + 1)
                if kind == "c":
                    if x >= 5:
                        act.wait_ge(pv_done, PV_BEFORE[x - 5] + 1)
                    nc.scalar.activation(pcT, banks[4][:, :], ACT.Copy).then_inc(copied, 1)
                    return
                n = HEAD_INDEX[x]
                if kind == "b" and n - 4 < HEAD_INDEX[FIRST_B]:
                    act.wait_ge(pv_done, PV_BEFORE[FIRST_B])
                elif n >= 4:
                    act.wait_ge(pv_done, PV_BEFORE[ITEM_OF[(n - 4) | 1]] + 1)
                for b, dst, cols in T_COPIES["b" if kind == "b" else "n"][0:2]:
                    dst_t = (pT_b if kind == "b" else pT)[n % 4]
                    nc.scalar.activation(dst_t[:, dst:dst + cols], banks[4 + b][:, 0:cols],
                                         ACT.Copy).then_inc(copied, 1)

            def out_hi(x):
                act.wait_ge(pv_done, PV_BEFORE[x] + 1)
                nc.scalar.activation(act_hi[:, ITEMS[x][1] // 2, :], banks[7][:, :], ACT.Copy)\
                  .then_inc(o_hi, 1)

            act.wait_ge(unit_done, N_IN)
            next_round = 1
            for x in range(N_ITEMS + 3):
                if x < N_ITEMS:
                    exps(x)
                    if next_round < ROUNDS and x == first_item(next_round - 1) + 2:
                        stack_hi_of(next_round)
                        next_round += 1
                if x == SPLIT_AT:
                    act.wait_ge(scored, 4 * first_item(ROUNDS - 1))
                    split_hi(OUT0)
                if 2 <= x <= N_ITEMS + 1:
                    copies(x - 2)
                if x - 3 in OUT_AFTER:
                    out_hi(x - 3)
                if x == N_ITEMS + 1:
                    act.wait_ge(scored, 4 * N_ITEMS)
                    split_hi(OUT0 + 1)

            def residual_tiles(n0):
                for n in range(n0, n0 + 4):
                    k, dst = RESIDUAL_ORDER[n]
                    if n >= 2:
                        act.wait_ge(act_lo_done, KT + n - 1)
                    nc.scalar.activation(ff_stage[:, n % 2, :], yT[:, k, :], ACT.Copy,
                                         scale=g_ffn[:, k:k + 1]).then_inc(xg_staged, 1)
                    act.wait_ge(xg_staged, KT + n + 1)
                    nc.scalar.activation(dst[0][:, k, :], ff_stage[:, n % 2, :], ACT.Copy)\
                      .then_inc(act_hi_done, 1)

            for step in range(OUT0 + 2, OUT0 + N_OUT + 2):
                split_hi(step)
                if step == OUT0 + 6:
                    residual_tiles(0)
                if step == OUT0 + N_OUT + 1:
                    act.wait_ge(unit_done, FF0)
                    residual_tiles(4)
                if step >= OUT0 + 5 and (step - 2 - OUT0) % 4 == 3:
                    q = (step - 2 - OUT0) // 4
                    for c in range(4 * q, 4 * q + 4):
                        act.wait_ge(bank_read, ALL_READ + c + 1)
                        if c >= 2:
                            act.wait_ge(square_added, KT + c - 1)
                        nc.scalar.activation(square[c % 2], yT[:, c, :], ACT.Square)\
                          .then_inc(squared, 1)

            def silu(base, i=0):
                for t in range(4):
                    act.wait_ge(bank_read, base + t + 1 + i * READ_PER_BLOCK)
                    nc.scalar.activation(ff_gate[:, t, :], ff_gate[:, t, :], ACT.Silu)\
                      .then_inc(gate_silu, 1)

            def ff_hi_of(base, i=0, dst=ff_hi):
                for t in range(4):
                    act.wait_ge(ff_staged, base + t + 1 + i * 4)
                    nc.scalar.activation(dst[:, t, :], ff_stage[:, t % 3, :], ACT.Copy)\
                      .then_inc(ff_hi_done, 1)

            for c in (2, 3, 4):
                residual_tiles(4 * c)
                split_hi(FF0 + c)
            root(2)
            split_hi(FF0 + 5)
            silu(OUT_READ)
            split_hi(FF0 + 6)
            split_hi(FF0 + 7)
            with act.Fori(0, LOOPS) as i:
                for j in range(PER_BLOCK):
                    split_hi(LOOP0 + j, i, PER_BLOCK)
                    if j == 1:
                        ff_hi_of(0, i)
                    if j == 5:
                        silu(OUT_READ + 4, i)
            for j in range(16):
                split_hi(TAIL0 + j)
                if j == 1:
                    ff_hi_of(4 * LOOPS)
                if j == 5:
                    silu(READ_TAIL)
                if j == 9:
                    ff_hi_of(4 * LOOPS + 4, dst=act_hi)
            for q in range(4):
                for i in range(TT):
                    act.wait_ge(out_transposed, 4 * q + i + 1)
                    if 4 * q + i >= 2:
                        act.wait_ge(out_squared, 4 * q + i - 1)
                    nc.scalar.activation(work[:, 512 * (i % 2):512 * (i % 2) + 512],
                                         SETS[q % 2][i][:, :], ACT.Square,
                                         accum_out=squares_by_row[:, i, q:q + 1])\
                      .then_inc(out_squared, 1)
            act.wait_ge(mean_ready, 3)
            nc.scalar.activation(stats[:, 1, 0, :], stats[:, 0, 0, :], ACT.Sqrt)\
              .then_inc(out_root, 1)
            act.wait_ge(out_rstd, 1)
            act.wait_ge(out_copied, 16)
            for i in (2, 3):
                nc.scalar.activation(out_rows[:, i, :], out_rows[:, i, :], ACT.Copy,
                                     scale=stats[:, 0, 1, i:i + 1]).then_inc(out_scaled[1], 1)

        @block.vector
        def _(dve):
            chain = [0]

            def then(ins):
                chain[0] += 1
                ins.then_inc(dve_chain, 1)
                dve.wait_ge(dve_chain, chain[0])

            def split_lo(step, i=0, per=0):
                kt, cols = unit_at(step)
                dve.wait_ge(hi_done, step + 1 + per * i)
                n = kt * cols
                nc.vector.tensor_tensor(w_lo[:, step % RING, 0:n], raw[:, step % RAW, 0:n],
                                        w_hi[:, step % RING, 0:n].bitcast(F32), ALU.subtract)\
                  .then_inc(lo_done, 1)

            def add_square(k, n):
                dve.wait_ge(squared, n + 1)
                if k == 0:
                    nc.vector.tensor_copy(sumsq, square[n % 2]).then_inc(square_added, 1)
                else:
                    dve.wait_ge(square_added, n)
                    nc.vector.tensor_tensor(sumsq, sumsq, square[n % 2], ALU.add)\
                      .then_inc(square_added, 1)

            def input_tiles(c):
                for k in range(4 * c, 4 * c + 4):
                    dve.wait_ge(act_hi_done, k + 1)
                    nc.vector.tensor_tensor(act_lo[:, k, :], xg_stage[k % 2],
                                            act_hi[:, k, :].bitcast(F32), ALU.subtract)\
                      .then_inc(act_lo_done, 1)
                    add_square(k, k)

            def newton(mean, root_of, y, t, made=None):
                then(nc.vector.reciprocal(y, root_of))
                then(nc.vector.tensor_tensor(t, y, y, ALU.mult))
                then(nc.vector.tensor_tensor(t, t, mean, ALU.mult))
                then(nc.vector.tensor_scalar(t, t, -0.5, 1.5, ALU.mult, ALU.add))
                if made is None:
                    then(nc.vector.tensor_tensor(y, y, t, ALU.mult))
                else:
                    nc.vector.tensor_tensor(y, y, t, ALU.mult).then_inc(made, 1)
                    dve.wait_ge(made, 1)

            def mean_square(bank, n):
                dve.wait_ge(sum_ready, n)
                dve.wait_ge(square_added, KT * n)
                nc.vector.tensor_scalar(sumsq, bank[:, :], 1.0 / D_MODEL, RMS_EPS, ALU.mult, ALU.add)\
                  .then_inc(mean_ready, 1)

            def rstd_of(n):
                dve.wait_ge(mean_ready, n)
                dve.wait_ge(root_ready, n)
                newton(sumsq, square[0], rstd, square[1])

            def scale_group(g):
                dve.wait_ge(unit_done, IN_LAST[g] + 1)
                if IN_RUNS[g][2] in (K_S, K_W):
                    dve.wait_ge(prep_pe, PREP["hidden0" if IN_RUNS[g][2] == K_S else "hidden1"])
                if IN_RUNS[g][2] == K_B:
                    for s in range(2):
                        dve.wait_ge(x_saved[s], 16 * KT // 2)
                for t in range(IN_TILES[g]):
                    nc.vector.tensor_tensor(tile_of(IN_RUNS[g][2] + t), SETS[g % 2][t][:, :], rstd,
                                            ALU.mult).then_inc(bank_read, 1)

            nc.vector.memset(ones[:, :], 1.0).then_inc(ones_made, 1)
            nc.vector.memset(kc_hi[:, :, :].bitcast(F32), 0.0).then_inc(ones_made, 1)
            nc.vector.memset(kc_lo[:, :, :].bitcast(F32), 0.0).then_inc(ones_made, 1)
            dve.wait_ge(setup_pe, 1)
            nc.vector.tensor_copy(vecs[:, :], banks[0][:, 0:P]).then_inc(vecs_ready, 1)
            input_tiles(0)
            split_lo(0)
            dve.wait_ge(setup_pe, 2)
            nc.vector.tensor_scalar(rel_t, banks[1][0:HEADS, 0:NUM_BUCKETS], -1.0, None, ALU.mult)\
              .then_inc(rel_read, 1)
            dve.wait_ge(rel_read, 1)
            then(nc.vector.memset(bias_rows[:, 0:2 * BIAS_W], MASKED))
            bucket = bucket_of_distance()
            runs = []
            for b in sorted(set(bucket.tolist())):
                ds = np.flatnonzero(bucket == b)
                runs.append((b, int(ds[0]), int(ds[-1])))
            for b, d0, d1 in runs:
                n = d1 - d0 + 1
                last = nc.vector.tensor_copy(bias_rows[:, SEQ - 1 - d1:SEQ - d0],
                                             rel_t[:, b:b + 1].to_broadcast([HEADS, n]))
            last.then_inc(bias_built, 1)
            for b, d0, d1 in runs:
                d1 = min(d1, SWA_WINDOW - 1)
                if d0 <= d1:
                    n = d1 - d0 + 1
                    last = nc.vector.tensor_copy(
                        bias_rows[:, BIAS_W + SEQ - 1 - d1:BIAS_W + SEQ - d0],
                        rel_t[:, b:b + 1].to_broadcast([HEADS, n]))
            last.then_inc(bias_built, 1)
            dve.wait_ge(rel_in, 16 * 2)
            nc.vector.tensor_scalar(sink_sb[:, 1, :], sink_sb[:, 0, :], -1.0, None, ALU.mult)\
              .then_inc(ones_made, 1)
            for c in range(1, 4):
                input_tiles(c)
                split_lo(c)
            mean_square(SETS[1][0], 1)
            split_lo(4)
            rstd_of(1)
            def make_blocks(s):
                for t in range(2):
                    for half in range(2):
                        src = tile_of((K_C, V_C)[s] + t)[64 * half:64 * half + 64, :]
                        for lp in range(2):
                            for jj in range(2):
                                v = src[:, CMP_STRIDE * jj + lp:]
                                v = bass.AP(src.tensor, v.offset,
                                            [list(src.ap[0]), [2, 8], [CMP_STRIDE, N_CMP]])
                                pv = pos[s][64 * half:64 * half + 64, :]
                                pv = bass.AP(pv.tensor, pv.offset + CMP_STRIDE * jj + lp,
                                             [list(pv.ap[0]), [2, 8], [0, N_CMP]])
                                last = nc.vector.tensor_tensor(
                                    blocks[s][64 * lp:64 * lp + 64, 8 * jj:8 * jj + 8, 2 * t + half, :],
                                    v, pv, ALU.add)
                last.then_inc(blocks_made, 1)

            def prepare(step):
                if step in (6, 7):
                    dve.wait_ge(biased, IN_TILES[0])
                    make_blocks(step - 6)
                elif step == 10:
                    then(nc.vector.memset(hid_v, 0.0))
                    then(nc.vector.memset(vc_pad, 0.0))
                    then(nc.vector.memset(score_c, MASKED))
                elif step == 12:
                    dve.wait_ge(prep_pe, PREP["hidT0"])
                    nc.vector.tensor_copy(hid_k, banks[5][:, 0:2 * ROWS_C].rearrange(
                        "p (k n) -> p k n", k=2)).then_inc(hid_copied, 1)
                elif step == 15:
                    dve.wait_ge(gate_exp, 1)
                    g_rows = tile_of(GATE)[0:N_GATES, :]
                    then(nc.vector.tensor_scalar(g_rows, g_rows, 1.0, None, ALU.add))
                    nc.vector.reciprocal(g_rows, g_rows).then_inc(gate_made, 1)
                elif step == 18:
                    dve.wait_ge(prep_pe, PREP["hidT1"])
                    for k in range(2):
                        for r in range(4):
                            last = nc.vector.tensor_copy(
                                hid_v[:, k, :, r, 0:N_CMP],
                                banks[0][:, ROWS_C * k:ROWS_C * (k + 1)].rearrange(
                                    "p (h n) -> p h n", h=NSA_KV))
                    last.then_inc(hid_copied, 1)
                    dve.wait_ge(prep_pe, PREP["kc"])
                    dve.wait_ge(ones_made, 4)
                    kc_ps = banks[1][:, 0:ROWS_C].rearrange("p (h n) -> p h n", h=NSA_KV)
                    then(nc.vector.tensor_copy(kc_hi[:, :, 0:N_CMP], kc_ps))
                    nc.vector.tensor_tensor(kc_lo[:, :, 0:N_CMP], kc_ps,
                                            kc_hi[:, :, 0:N_CMP].bitcast(F32), ALU.subtract)\
                      .then_inc(kc_made, 1)
                    dve.wait_ge(prep_pe, PREP["gates"])
                    dve.wait_ge(valid_made, 1)
                    then(nc.vector.tensor_copy(gates[:, :, :].rearrange("p i g -> p (i g)"),
                                               banks[2][:, 0:TT * N_GATES]))
                    g_c = gates[:, 0, :].rearrange("p (h b) -> p h b", b=3)[:, :, 0:1]
                    nc.vector.tensor_scalar(g_c, g_c, valid[:, 0:1], None, ALU.mult)\
                      .then_inc(gate_made, 1)
                elif step == 19:
                    dve.wait_ge(prep_pe, PREP["vc"])
                    for h in range(4):
                        last = nc.vector.tensor_copy(
                            vc_pad[32 * h:32 * h + 32, :, h, :],
                            banks[3][32 * h:32 * h + 32, 0:NSA_KV * HEAD_DIM].rearrange(
                                "p (k d) -> p k d", k=NSA_KV))
                    last.then_inc(kc_made, 1)
                elif step in (22, 26):
                    for n, t, bank in V_TILES:
                        if (t == V_B) == (step == 26):
                            dve.wait_ge(prep_pe, PREP[f"v{n}"])
                            nc.vector.tensor_copy(tile_of(t), bank[:, :]).then_inc(v_copied, 1)
                elif step == N_IN:
                    nc.vector.memset(prob_c, 0.0).then_inc(prep_done, 1)
                    stack_lo_of(0)

            def stack_lo_of(r):
                if r >= 2:
                    dve.wait_ge(scored, 4 * first_item(r - 1))
                for n, src, hi, dst, scale in stack_sources(r)[1]:
                    dve.wait_ge(stack_hi, STACK_BEFORE[r] + n)
                    nc.vector.scalar_tensor_tensor(dst, src, scale, hi.bitcast(F32), ALU.mult,
                                                   ALU.subtract).then_inc(stack_lo, 1)

            def mask_scores(x):
                kind, h = ITEMS[x]
                if kind == "c":
                    dve.wait_ge(scored, 4 * x + 4)
                    for o in range(2):
                        dve.wait_ge(table_in[(h + o) % 4], 16 * (h // 4 + 1))
                    if x >= 5:
                        dve.wait_ge(transposed, x - 4)
                    ps = banks[0][:, 0:256].rearrange("p (i h c) -> p i h c", i=TT, h=2)
                    for i in range(TT):
                        n = 8 * i + 7
                        tab = tables[:, h % 4:h % 4 + 2, :]
                        tab = bass.AP(tab.tensor, tab.offset + SEQ - P - P * i + CMP_LEN - 1,
                                      [list(tab.ap[0]), [SEQ, 2], [CMP_STRIDE, n]])
                        last = nc.vector.tensor_tensor(score_c[:, i, :, 0:n], ps[:, i, :, 0:n], tab,
                                                       ALU.add)
                        if i < TT - 1:
                            last.then_inc(masked, 1)
                    then(last)
                    least = cstats[:, 0, :].rearrange("p (i h) -> p i h", i=TT)
                    then(nc.vector.tensor_reduce(least, score_c, AX.X, ALU.min))
                    nc.vector.tensor_tensor(
                        prob_c[:, :, h % 4:h % 4 + 2, :],
                        least.unsqueeze(3).to_broadcast([P, TT, 2, 32]), score_c, ALU.subtract)\
                      .then_inc(masked, 1)
                    return
                n = HEAD_INDEX[x]
                if kind != "w":
                    dve.wait_ge(table_in[h % 4], 16 * (h // 4 + 1))
                if n >= 3:
                    dve.wait_ge(transposed, ITEM_OF[n - 3] + 1)
                if n >= 4:
                    dve.wait_ge(normed, NORM_BEFORE[ITEM_OF[n - 4]] + 3)
                    dve.wait_ge(last_normed, n - 3)
                for i in range(TT):
                    off, keys = key_columns(kind, i)
                    cols = P * len(keys)
                    dve.wait_ge(scored, 4 * x + i + 1)
                    first = banks[i][:, 0:cols]
                    init = 3e38
                    tab = tables[:, h % 4, SEQ - cols:SEQ]
                    if kind == "b":
                        init = sink_sb[:, 1, h - NSA_HEADS:h - NSA_HEADS + 1]
                        tab = tables_b[:, h % 4, 2 * P - cols:2 * P]
                    nc.vector.tensor_tensor_reduce(
                        prob[n % 3][:, off:off + cols], first, tab, 1.0, init, ALU.add, ALU.min, stats[:, n % 4, 0, i:i + 1])\
                      .then_inc(masked, 1)

            def normalise(x):
                kind, h = ITEMS[x]
                if kind == "c":
                    p = prob_c[:, :, h % 4:h % 4 + 2, :]
                    dve.wait_ge(exped, EXP_BEFORE[x] + 1)
                    total = cstats[:, 1, :].rearrange("p (i h) -> p i h", i=TT)
                    rec = cstats[:, 2, :].rearrange("p (i h) -> p i h", i=TT)
                    then(nc.vector.tensor_reduce(total, p, AX.X, ALU.add))
                    then(nc.vector.reciprocal(rec, total))
                    g = gates[:, :, 3 * h:3 * h + 6].rearrange("p i (h b) -> p i h b", b=3)[:, :, :, 0]
                    then(nc.vector.tensor_tensor(rec, rec, g, ALU.mult))
                    nc.vector.tensor_tensor(p, p, rec.unsqueeze(3).to_broadcast([P, TT, 2, 32]),
                                            ALU.mult).then_inc(normed, 1)
                    return
                n = HEAD_INDEX[x]
                dve.wait_ge(exped, EXP_BEFORE[x] + (5 if kind == "b" else 4))
                total, rec = stats[:, n % 4, 1, :], stats[:, n % 4, 2, :]
                if kind == "b":
                    then(nc.vector.tensor_tensor(total, total, rec, ALU.add))
                    last = nc.vector.reciprocal(rec, total)
                else:
                    then(nc.vector.reciprocal(rec, total))
                    g = 3 * h + (1 if kind == "s" else 2)
                    last = nc.vector.tensor_tensor(rec, rec, gates[:, :, g], ALU.mult)
                last.then_inc(factor_made, 1)
                dve.wait_ge(factor_made, n + 1)
                for i in range(TT - 1):
                    off, keys = key_columns(kind, i)
                    p = prob[n % 3][:, off:off + P * len(keys)]
                    nc.vector.tensor_scalar(p, p, rec[:, i:i + 1], None, ALU.mult)\
                      .then_inc(normed, 1)

            def copy_third(x):
                n = HEAD_INDEX[x]
                dve.wait_ge(transposed, x + 1)
                if n >= 4:
                    dve.wait_ge(pv_done, PV_BEFORE[ITEM_OF[(n - 4) | 1]] + 1)
                b, dst, cols = T_COPIES["n"][2]
                nc.vector.tensor_copy(pT[n % 4][:, dst:dst + cols], banks[4 + b][:, 0:cols])\
                  .then_inc(third_copied, 1)

            def out_lo(x):
                m = OUT_AFTER.index(x)
                dve.wait_ge(o_hi, m + 1)
                t = ITEMS[x][1] // 2
                nc.vector.tensor_tensor(act_lo[:, t, :], banks[7][:, :],
                                        act_hi[:, t, :].bitcast(F32), ALU.subtract)\
                  .then_inc(o_lo, 1)

            for step in range(5, N_IN + 2):
                if step < N_IN:
                    split_lo(step)
                if step - 2 in IN_LAST:
                    scale_group(IN_LAST.index(step - 2))
                prepare(step)

            dve.wait_ge(kc_made, 2)
            dve.wait_ge(gate_made, 2)
            next_round = 1
            for x in range(N_ITEMS + 3):
                if x < N_ITEMS:
                    mask_scores(x)
                if 1 <= x <= N_ITEMS:
                    normalise(x - 1)
                if 2 <= x <= N_ITEMS + 1 and ITEMS[x - 2][0] in "sw":
                    copy_third(x - 2)
                if x < N_ITEMS and next_round < ROUNDS and x == first_item(next_round - 1) + 2:
                    stack_lo_of(next_round)
                    next_round += 1
                if x == SPLIT_AT:
                    split_lo(OUT0)
                if x - 3 in OUT_AFTER:
                    out_lo(x - 3)
                if x == N_ITEMS + 1:
                    split_lo(OUT0 + 1)

            def residual_tiles(n0):
                for n in range(n0, n0 + 4):
                    k, dst = RESIDUAL_ORDER[n]
                    dve.wait_ge(act_hi_done, KT + n + 1)
                    nc.vector.tensor_tensor(dst[1][:, k, :], ff_stage[:, n % 2, :],
                                            dst[0][:, k, :].bitcast(F32), ALU.subtract)\
                      .then_inc(act_lo_done, 1)

            for step in range(OUT0 + 2, OUT0 + N_OUT + 2):
                split_lo(step)
                if step == OUT0 + 6:
                    residual_tiles(0)
                if step == OUT0 + N_OUT + 1:
                    residual_tiles(4)
                if step >= OUT0 + 5 and (step - 2 - OUT0) % 4 == 3:
                    q = (step - 2 - OUT0) // 4
                    dve.wait_ge(unit_done, step - 1)
                    dve.wait_ge(y_in, 16)
                    for t in range(4):
                        nc.vector.tensor_tensor(yT[:, 4 * q + t, :], yT[:, 4 * q + t, :],
                                                SETS[(OUT_GROUP0 + q) % 2][t][:, :], ALU.add)\
                          .then_inc(bank_read, 1)
                    for c in range(4 * q, 4 * q + 4):
                        add_square(c, KT + c)

            def gate_out(group, base_unit, i=0):
                dve.wait_ge(unit_done, base_unit + PER_BLOCK * i)
                for t in range(4):
                    nc.vector.tensor_tensor(ff_gate[:, t, :], SETS[group % 2][t][:, :], rstd, ALU.mult)\
                      .then_inc(bank_read, 1)

            def ff_out(group, base_unit, base, i=0, dst=(ff_hi, ff_lo)):
                dve.wait_ge(unit_done, base_unit + PER_BLOCK * i)
                for t in range(5):
                    if t < 4:
                        dve.wait_ge(gate_ready, base + t + 1 + i * 4)
                        if t == 3:
                            dve.wait_ge(ff_lo_done, base + 1 + i * 4)
                        nc.vector.tensor_tensor(ff_stage[:, t % 3, :], SETS[group % 2][t][:, :],
                                                ff_gate[:, t, :], ALU.mult).then_inc(ff_staged, 1)
                    if t >= 1:
                        dve.wait_ge(ff_hi_done, base + t + i * 4)
                        nc.vector.tensor_tensor(dst[1][:, t - 1, :], ff_stage[:, (t - 1) % 3, :],
                                                dst[0][:, t - 1, :].bitcast(F32), ALU.subtract)\
                          .then_inc(ff_lo_done, 1)

            def down_out(group, base_unit, q, i=0):
                dve.wait_ge(unit_done, base_unit + PER_BLOCK * i)
                for t in range(4):
                    nc.vector.tensor_tensor(yT[:, 4 * q + t, :], yT[:, 4 * q + t, :],
                                            SETS[group % 2][t][:, :], ALU.add)\
                      .then_inc(bank_read, 1)

            for c in (2, 3, 4):
                residual_tiles(4 * c)
                split_lo(FF0 + c)
            mean_square(SETS[(FF_GROUP0 + 1) % 2][0], 2)
            rstd_of(2)
            split_lo(FF0 + 5)
            gate_out(FF_GROUP0, FF0 + 4)
            split_lo(FF0 + 6)
            split_lo(FF0 + 7)
            with dve.Fori(0, LOOPS) as i:
                for j in range(PER_BLOCK):
                    split_lo(LOOP0 + j, i, PER_BLOCK)
                    done = LOOP0 + j - 1
                    if j == 1:
                        ff_out(LOOP_GROUP0 - 1, done, 0, i)
                    if j == 5:
                        gate_out(LOOP_GROUP0, done, i)
                    if j >= 6 and j < 10:
                        down_out(LOOP_GROUP0 + j - 5, done, j - 6, i)
            for j in range(18):
                if j < 16:
                    split_lo(TAIL0 + j)
                done = TAIL0 + j - 1
                if j == 1:
                    ff_out(TAIL_GROUP0 - 1, done, 4 * LOOPS)
                if j == 5:
                    gate_out(TAIL_GROUP0, done)
                if j == 9:
                    ff_out(TAIL_GROUP0 + 1, done, 4 * LOOPS + 4, dst=(act_hi, act_lo))
                if j >= 10:
                    down_out(TAIL_GROUP0 + j - 8, done, (j - 10) % 4)
            dve.wait_ge(g_final_in, 16)
            for q in range(4):
                for i in range(TT):
                    dve.wait_ge(out_squared, 4 * q + i + 1)
                    cols = slice(UNIT_COLS * q, UNIT_COLS * (q + 1))
                    nc.vector.tensor_tensor(out_rows[:, i, cols], SETS[q % 2][i][:, :],
                                            g_final[:, cols], ALU.mult).then_inc(out_copied, 1)
            mean, rows_rstd, t = stats[:, 0, 0, :], stats[:, 0, 1, :], stats[:, 0, 2, :]
            then(nc.vector.tensor_reduce(mean, squares_by_row[:, :, :], AX.X, ALU.add))
            nc.vector.tensor_scalar(mean, mean, 1.0 / D_MODEL, RMS_EPS, ALU.mult, ALU.add)\
              .then_inc(mean_ready, 1)
            dve.wait_ge(mean_ready, 3)
            dve.wait_ge(out_root, 1)
            newton(mean, stats[:, 1, 0, :], rows_rstd, t, out_rstd)
            dve.wait_ge(out_copied, 16)
            for i in (0, 1):
                nc.vector.tensor_scalar(out_rows[:, i, :], out_rows[:, i, :], rows_rstd[:, i:i + 1],
                                        None, ALU.mult).then_inc(out_scaled[0], 1)

        @block.tensor
        def _(pe):
            def unit(step, x_hi, x_lo, dst, first, last, i=0, per=0, kt=UNIT_KT, cols=UNIT_COLS):
                pe.wait_ge(lo_done, step + 1 + per * i)
                wh = w_hi[:, step % RING, 0:kt * cols].rearrange("p (t c) -> p t c", t=kt)
                wl = w_lo[:, step % RING, 0:kt * cols].rearrange("p (t c) -> p t c", t=kt)
                for t in range(kt):
                    for c in range(cols // P):
                        cs = slice(P * c, P * (c + 1))
                        start, stop = first and t == 0, last and t == kt - 1
                        nc.tensor.matmul(dst[c][:, :], wh[:, t, cs], x_lo(t), start=start, stop=False)
                        nc.tensor.matmul(dst[c][:, :], wl[:, t, cs], x_hi(t), start=False, stop=False)
                        done = nc.tensor.matmul(dst[c][:, :], wh[:, t, cs], x_hi(t), start=False,
                                                stop=stop)
                done.then_inc(unit_done, 1)

            def act_unit(step, k0, dst, kt=UNIT_KT, cols=UNIT_COLS, i=0, per=0):
                unit(step, lambda t: act_hi[:, k0 + t, :], lambda t: act_lo[:, k0 + t, :], dst,
                     k0 == 0, k0 + kt == KT, i, per, kt, cols)

            def in_unit(step):
                g, k, kt, _, n, _ = IN_UNITS[step]
                if g == 0:
                    pe.wait_ge(act_lo_done, k + kt)
                if k == 0 and g >= 2:
                    pe.wait_ge(bank_read, tiles_before(g - 1))
                act_unit(step, k, SETS[g % 2], kt, n)

            def transpose_input(c):
                pe.wait_ge(x_in[c % 2], 16 * (c // 2 + 1))
                for k in range(4 * c, 4 * c + 4):
                    if k >= 4:
                        pe.wait_ge(xg_staged, k - 3)
                    for i in range(TT):
                        t = nc.tensor.transpose(SETS[1][k % 4][:, P * i:P * (i + 1)],
                                                x_chunk[c % 2][:, i, P * (k % 4):P * (k % 4 + 1)],
                                                ident[:, :])
                    t.then_inc(xT_ready, 1)

            def sum_squares(bank, n):
                pe.wait_ge(square_added, KT * n)
                nc.tensor.matmul(bank[:, :], ones[:, :], sumsq, start=True, stop=True)\
                  .then_inc(sum_ready, 1)

            def prepare(name):
                kind, s = name.rstrip("01234"), int(name[-1]) if name[-1].isdigit() else 0
                if kind == "hidden":
                    pe.wait_ge(w1_in[s], 16)
                    pe.wait_ge(blocks_made, s + 1)
                    for j in range(16):
                        last = nc.tensor.matmul(banks[4 * s][0:ROWS_C, 0:CMP_HIDDEN],
                                                blocks[s][:, j, :, :].rearrange("p h n -> p (h n)"),
                                                w1[s][:, j, :], start=j == 0, stop=j == 15)
                elif kind == "hidT":
                    pe.wait_ge(gelu_done, s + 1)
                    for k in range(2):
                        last = nc.tensor.transpose(
                            banks[(5, 0)[s]][:, ROWS_C * k:ROWS_C * (k + 1)],
                            hidden[s][:, P * k:P * (k + 1)], ident[0:ROWS_C, 0:ROWS_C])
                elif kind == "kc":
                    pe.wait_ge(hid_copied, 1)
                    pe.wait_ge(w2_in, 16 * 3)
                    for k in range(2):
                        last = nc.tensor.matmul(banks[1][:, 0:ROWS_C],
                                                w2k[:, k, :, :].rearrange("p r d -> p (r d)"),
                                                hid_k[:, k, :], start=k == 0, stop=k == 1)
                elif kind == "gates":
                    pe.wait_ge(gate_made, 1)
                    for j in range(TT):
                        last = nc.tensor.transpose(banks[2][:, N_GATES * j:N_GATES * (j + 1)],
                                                   tile_of(GATE)[0:N_GATES, P * j:P * (j + 1)],
                                                   ident[0:N_GATES, 0:N_GATES])
                elif kind == "vc":
                    pe.wait_ge(hid_copied, 2)
                    for h in range(NSA_KV):
                        for k in range(2):
                            last = nc.tensor.matmul(banks[3][:, HEAD_DIM * h:HEAD_DIM * (h + 1)],
                                                    hid_v[:, k, h, :, :].rearrange("p r c -> p (r c)"),
                                                    w2v[:, k, :], start=k == 0, stop=k == 1)
                else:
                    _, t, bank = V_TILES[s]
                    pe.wait_ge(biased, tiles_before(5))
                    for j in range(TT):
                        last = nc.tensor.transpose(bank[:, P * j:P * (j + 1)],
                                                   tile_of(t)[:, P * j:P * (j + 1)], ident[:, :])
                last.then_inc(prep_pe, 1)

            pe.wait_ge(ident_made, 1)
            transpose_input(0)
            pe.wait_ge(consts_in, 16 * CONSTS)
            nc.tensor.transpose(banks[0][:, 0:P], vec_rows, ident[:, :]).then_inc(setup_pe, 1)
            pe.wait_ge(rel_in, 16 * 2)
            nc.tensor.transpose(banks[1][0:HEADS, 0:NUM_BUCKETS], rel_rows,
                                ident[0:NUM_BUCKETS, 0:NUM_BUCKETS]).then_inc(setup_pe, 1)
            transpose_input(1)
            pe.wait_ge(vecs_ready, 1)
            pe.wait_ge(rel_read, 1)
            in_unit(0)
            transpose_input(2)
            in_unit(1)
            transpose_input(3)
            in_unit(2)
            pe.wait_ge(ones_made, 1)
            pe.wait_ge(xg_staged, KT)
            sum_squares(SETS[1][0], 1)
            in_unit(3)
            pe.wait_ge(mean_ready, 1)
            for step in range(4, N_IN):
                if step == 8:
                    pe.wait_ge(gelu_done, 1)
                if step == 12:
                    pe.wait_ge(gelu_done, 2)
                if step == 15:
                    pe.wait_ge(hid_copied, 1)
                if step == 19:
                    pe.wait_ge(kc_made, 2)
                    pe.wait_ge(gate_made, 2)
                if step == 23:
                    pe.wait_ge(v_copied, 4)
                if step == 27:
                    pe.wait_ge(v_copied, 5)
                in_unit(step)
                for name in PREP_AFTER.get(step, ()):
                    pe.wait_ge(bank_read, tiles_before(IN_UNITS[step][0]))
                    prepare(name)

            def score(x):
                kind, h = ITEMS[x]
                slot = (h // 4 + 1) % 2
                if x == first_item(h // 4):
                    pe.wait_ge(stack_lo, STACK_BEFORE[h // 4 + 1])

                def queries(head, i):
                    at = SEQ * (head % 4) + P * i
                    return w_hi[:, slot, at:at + P]

                if kind == "c":
                    if x >= 1:
                        pe.wait_ge(masked, 4 * (x - 1) + 1)
                    for i in range(TT):
                        for e in range(2):
                            at = 64 * i + 32 * e
                            nc.tensor.matmul(banks[0][:, at:at + 32], queries(h + e, i),
                                             kc_lo[:, h // 4, :], start=True, stop=False)
                            last = nc.tensor.matmul(banks[0][:, at:at + 32], queries(h + e, i),
                                                    kc_hi[:, h // 4, :], start=False, stop=True)
                        last.then_inc(scored, 1)
                    return
                k_hi = 2 * SEQ if kind == "w" else 0
                for i in range(TT):
                    if ITEMS[x - 1][0] != "c":
                        pe.wait_ge(masked, 4 * (x - 1) + i + 1)
                    elif i == 0:
                        pe.wait_ge(masked, 4 * x)
                    elif x >= 2:
                        pe.wait_ge(masked, 4 * (x - 2) + i + 1)
                    k0 = max(0, P * (i - 1)) if kind == "b" else 0
                    n = 2 * P if kind == "b" else max(2 * P, P * (i + 1))
                    for at in (k_hi + SEQ, k_hi):
                        last = nc.tensor.matmul(banks[i][:, 0:n], queries(h, i),
                                                w_lo[:, slot, at + k0:at + k0 + n],
                                                start=at != k_hi, stop=at == k_hi)
                    last.then_inc(scored, 1)

            def transpose_probs(x):
                kind, h = ITEMS[x]
                pe.wait_ge(copied, COPY_BEFORE[x])
                if THIRD_BEFORE[x]:
                    pe.wait_ge(third_copied, THIRD_BEFORE[x])
                if kind == "c":
                    pe.wait_ge(normed, NORM_BEFORE[x] + 1)
                    for i in range(TT):
                        last = nc.tensor.transpose(
                            banks[4][:, P * i:P * (i + 1)],
                            prob_c[:, i, :, :].rearrange("p h c -> p (h c)"), ident[:, :])
                    last.then_inc(transposed, 1)
                    return
                n = HEAD_INDEX[x]
                where = T_BANK["b" if kind == "b" else "n"]
                for i in range(TT):
                    if i < TT - 1:
                        pe.wait_ge(normed, NORM_BEFORE[x] + i + 1)
                    else:
                        pe.wait_ge(last_normed, n + 1)
                    off, keys = key_columns(kind, i)
                    for m, j in enumerate(keys):
                        b, col = where[j]
                        col += P * (i - j)
                        last = nc.tensor.transpose(banks[4 + b][:, col:col + P],
                                                   prob[n % 3][:, off + P * m:off + P * (m + 1)],
                                                   ident[:, :])
                last.then_inc(transposed, 1)

            def products(x):
                kind, h = ITEMS[x]
                h -= h % 2
                pe.wait_ge(copied, COPY_BEFORE[x + 1])
                if THIRD_BEFORE[x + 1]:
                    pe.wait_ge(third_copied, THIRD_BEFORE[x + 1])
                if kind in "cb":
                    pe.wait_ge(o_lo, sum(y < x for y in OUT_AFTER))
                if kind == "c":
                    for e in range(2):
                        last = nc.tensor.matmul(banks[7][64 * e:64 * e + 64, :],
                                                vc_pad[:, h // 4, h % 4 + e, :], pcT, start=True,
                                                stop=False, skip_group_check=True)
                    last.then_inc(pv_done, 1)
                    return
                n = HEAD_INDEX[x]
                kv = (h - NSA_HEADS) // 8 if kind == "b" else h // 4
                v = tile_of({"s": V_S, "w": V_W, "b": V_B}[kind] + (0 if kind == "b" else kv // 2))
                for j in range(TT):
                    cols = min(2 * P, SEQ - P * j) if kind == "b" else SEQ - P * j
                    at = T_SBUF["b" if kind == "b" else "n"][j]
                    for e in range(2):
                        slot = (n - 1 + e) % 4
                        vcol = P * j + 64 * (kv % 2)
                        last = nc.tensor.matmul(
                            banks[7][64 * e:64 * e + 64, P * j:P * j + cols],
                            v[:, vcol:vcol + 64], (pT_b if kind == "b" else pT)[slot][:, at:at + cols],
                            start=kind == "b" and j == 0, stop=kind != "s" and j == TT - 1,
                            skip_group_check=True)
                last.then_inc(pv_done, 1)

            def out_unit(n):
                q, k = n // 4, n % 4
                g = OUT_GROUP0 + q
                if q == 0:
                    pe.wait_ge(o_lo, 4 * k + 4)
                elif q >= 2 and k == 0:
                    pe.wait_ge(bank_read, tiles_before(g - 1))
                act_unit(OUT0 + n, 4 * k, SETS[g % 2])

            pe.wait_ge(bank_read, ALL_READ)
            pe.wait_ge(prep_done, 1)
            for x in range(N_ITEMS + 3):
                if x < N_ITEMS:
                    score(x)
                if 2 <= x <= N_ITEMS + 1:
                    transpose_probs(x - 2)
                if x == N_ITEMS + 1:
                    pe.wait_ge(masked, 4 * N_ITEMS)
                    out_unit(0)
                if x - 3 in PV_RUNS:
                    products(x - 3)
            for n in range(1, N_OUT):
                out_unit(n)

            pe.wait_ge(bank_read, tiles_before(FF_GROUP0 - 1))
            for k in range(4):
                pe.wait_ge(act_lo_done, KT + 4 * k + 4)
                if k == 0:
                    unit(FF0, lambda t: ff_hi[:, t, :], lambda t: ff_lo[:, t, :],
                         SETS[FF_GROUP0 % 2], True, False)
                else:
                    act_unit(FF0 + k, 4 * k, SETS[FF_GROUP0 % 2])
                if k == 2:
                    pe.wait_ge(bank_read, OUT_READ)
                    sum_squares(SETS[(FF_GROUP0 + 1) % 2][0], 2)
            pe.wait_ge(mean_ready, 2)
            pe.wait_ge(act_lo_done, KT + len(RESIDUAL_ORDER))
            for k in range(4):
                act_unit(FF0 + 4 + k, 4 * k, SETS[(FF_GROUP0 + 1) % 2])

            def down(step, group, i=0, per=0, x=(ff_hi, ff_lo)):
                unit(step, lambda t: x[0][:, t, :], lambda t: x[1][:, t, :], SETS[group % 2],
                     True, True, i, per)

            read0, read_per = OUT_READ + 4, READ_PER_BLOCK
            with pe.Fori(0, LOOPS) as i:
                pe.wait_ge(bank_read, read0 + read_per * i)
                for k in range(4):
                    act_unit(LOOP0 + k, 4 * k, SETS[LOOP_GROUP0 % 2], i=i, per=PER_BLOCK)
                pe.wait_ge(ff_lo_done, 4 * i + 4)
                for q in range(4):
                    if q:
                        pe.wait_ge(bank_read, read0 + 4 * q + read_per * i)
                    down(LOOP0 + 4 + q, LOOP_GROUP0 + 1 + q, i, PER_BLOCK)
                pe.wait_ge(bank_read, read0 + 16 + read_per * i)
                for k in range(4):
                    act_unit(LOOP0 + 8 + k, 4 * k, SETS[(LOOP_GROUP0 + 5) % 2], i=i, per=PER_BLOCK)
            pe.wait_ge(bank_read, READ_TAIL)
            for k in range(4):
                act_unit(TAIL0 + k, 4 * k, SETS[TAIL_GROUP0 % 2])
            pe.wait_ge(ff_lo_done, 4 * (FF_BLOCKS - 1))
            for k in range(4):
                act_unit(TAIL0 + 4 + k, 4 * k, SETS[(TAIL_GROUP0 + 1) % 2])
            for q in range(8):
                if q == 1:
                    pe.wait_ge(ff_staged, 4 * FF_BLOCKS)
                else:
                    pe.wait_ge(bank_read, READ_TAIL + 4 * max(1, q))
                if q == 4:
                    pe.wait_ge(ff_lo_done, 4 * FF_BLOCKS)
                down(TAIL0 + 8 + q, TAIL_GROUP0 + 2 + q,
                     x=(ff_hi, ff_lo) if q < 4 else (act_hi, act_lo))

            for q in range(4):
                pe.wait_ge(bank_read, READ_TAIL + 4 * 9)
                if q >= 2:
                    pe.wait_ge(out_copied, 4 * (q - 1))
                for i in range(TT):
                    for c in range(4):
                        last = nc.tensor.transpose(SETS[q % 2][i][:, P * c:P * (c + 1)],
                                                   yT[:, 4 * q + c, P * i:P * (i + 1)], ident[:, :])
                    last.then_inc(out_transposed, 1)


_INS = ["x", "rel_bias", "norm_mix", "norm_ffn", "w_in", "b_in", "cmp_pos_k", "cmp_pos_v",
        "cmp_k_w1", "cmp_k_w2", "cmp_v_w1", "cmp_v_w2", "sinks", "w_out", "w_gate", "w_up",
        "w_down", "norm_final"]


def kernel(**inputs):
    import concourse.bacc as bacc
    from concourse.bass_utils import run_bass_kernel_spmd

    nc = bacc.Bacc("TRN2", target_bir_lowering=False, num_devices=1)
    arrays, args = {}, {}
    for name in _INS:
        a = np.ascontiguousarray(inputs[name])
        arrays[f"in_{name}"] = a
        args[name] = nc.dram_tensor(f"in_{name}", a.shape, mybir.dt.from_np(a.dtype),
                                    kind="ExternalInput").ap()
    shape = inputs["x"].shape
    args["out"] = nc.dram_tensor("out_rows_dram", shape, F32, kind="ExternalOutput").ap()
    build(nc, **args)
    r = run_bass_kernel_spmd(nc, [arrays], core_ids=[0])
    return r.results[0]["out_rows_dram"]
```
